# Optimizing a Trainium2 kernel written in Bass

```python
import math
import jax
import jax.numpy as jnp
from jax import lax
import numpy as np

D_MODEL = 1024
BATCH = 1
SEQ = 128
DEPTH = 2
DEC_BATCH = 1
DEC_SEQ = 512
PAST_LEN = 128

GRID_W = 64
Q_BLOCK = 128
HEAD_DIM = 64
ROPE_BASE = 10000.0
EPS = 1e-6
NEG_INF = -1e30
A_HEADS = 4
A_QK = 32
A_V = 64
B_HEADS = 4
B_KV = 2
WINDOW = 128
C_HEADS = 4
C_KV = 2
D_HEADS = 4
D_Q_LORA = 256
D_KV_LORA = 128
D_NOPE = 64
D_ROPE = 32
D_V = 64
D_QK = D_NOPE + D_ROPE
N_BRANCH = 4
BRANCH_W = 256
PEER_HEADS = 8
PEER_KEYS = 128
PEER_EXPERTS = PEER_KEYS * PEER_KEYS
PEER_QDIM = 256
PEER_HALF = PEER_QDIM // 2
PEER_TOPK = 16
PEER_CHUNK = 128
IN_SIZES = (A_HEADS * 2 * A_QK, A_HEADS * 2 * A_QK, A_HEADS * A_V,
            B_HEADS * HEAD_DIM, B_KV * HEAD_DIM, B_KV * HEAD_DIM,
            C_HEADS * HEAD_DIM, C_KV * HEAD_DIM, C_KV * HEAD_DIM,
            D_Q_LORA, D_KV_LORA, D_ROPE, N_BRANCH * D_MODEL)
IN_COLS = sum(IN_SIZES)

kernel_name = 'hybrid_diffusion_prefix_trunk_step'

def _rms(x, g):
    x32 = x.astype(jnp.float32)
    y = x32 * lax.rsqrt(jnp.mean(x32 * x32, axis=-1, keepdims=True) + EPS)
    return y.astype(x.dtype) * g

def _axial_rope(x):
    T, d = x.shape[1], x.shape[-1]
    rows = T // GRID_W
    q4 = d // 4
    inv = ROPE_BASE ** (-jnp.arange(q4, dtype=jnp.float32) / q4)
    row = jnp.repeat(jnp.arange(rows, dtype=jnp.float32), GRID_W)
    col = jnp.tile(jnp.arange(GRID_W, dtype=jnp.float32), rows)
    ar = row[:, None] * inv
    ac = col[:, None] * inv
    ang = jnp.concatenate([ar, ar, ac, ac], axis=-1)
    shape = (1, T) + (1,) * (x.ndim - 3) + (d,)
    cos = jnp.cos(ang).reshape(shape)
    sin = jnp.sin(ang).reshape(shape)
    xr = x.reshape(x.shape[:-1] + (2, 2, q4))
    rot = jnp.stack([-xr[..., 1, :], xr[..., 0, :]], axis=-2).reshape(x.shape)
    return (x * cos + rot * sin).astype(x.dtype)

def _split_in(proj):
    offs = [int(o) for o in np.cumsum(IN_SIZES)[:-1]]
    return jnp.split(proj, offs, axis=-1)

def _to_blocks(x):
    B, T = x.shape[:2]
    return x.reshape((B, T // Q_BLOCK, Q_BLOCK) + x.shape[2:]).swapaxes(0, 1)

def _from_blocks(y):
    nb, B = y.shape[:2]
    return y.swapaxes(0, 1).reshape((B, nb * Q_BLOCK) + y.shape[3:])

def _attend(q, k, v, scale, bias=None, sink=None):
    s = jnp.einsum('bqhgd,bkhd->bhgqk', q, k).astype(jnp.float32) * scale
    if bias is not None:
        s = s + bias
    if sink is None:
        p = jax.nn.softmax(s, axis=-1)
    else:
        sk = sink.astype(jnp.float32)[None, :, :, None, None]
        m = jnp.maximum(jnp.max(s, axis=-1, keepdims=True), sk)
        e = jnp.exp(s - m)
        p = e / (jnp.sum(e, axis=-1, keepdims=True) + jnp.exp(sk - m))
    return jnp.einsum('bhgqk,bkhd->bqhgd', p.astype(v.dtype), v)

def _dense_gqa(q, k, v, scale, sink=None):
    B, T, H, d = q.shape
    n_kv = k.shape[2]
    qg = q.reshape(B, T, n_kv, H // n_kv, d)
    out = lax.map(lambda qb: _attend(qb, k, v, scale, sink=sink), _to_blocks(qg))
    return _from_blocks(out).reshape(B, T, H * v.shape[-1])

def _window_gqa(q, k_lat, v_lat, k_ctx, v_ctx, scale, sink):
    B, T, H, d = q.shape
    n_kv = k_lat.shape[2]
    nb = T // Q_BLOCK
    L = k_ctx.shape[1]

    def band(x):
        xp = jnp.pad(x, ((0, 0), (Q_BLOCK, Q_BLOCK), (0, 0), (0, 0)))
        xb = xp.reshape((B, nb + 2, Q_BLOCK) + x.shape[2:])
        xb = jnp.concatenate([xb[:, :-2], xb[:, 1:-1], xb[:, 2:]], axis=2)
        return xb.swapaxes(0, 1)

    kb, vb = band(k_lat), band(v_lat)
    r = jnp.arange(Q_BLOCK)
    cpos = jnp.arange(3 * Q_BLOCK)
    rel = cpos[None, :] - Q_BLOCK - r[:, None]

    def blk(args):
        qb, kbb, vbb, i = args
        kpos = (i - 1) * Q_BLOCK + cpos
        valid = (jnp.abs(rel) <= WINDOW) & ((kpos >= 0) & (kpos < T))[None, :]
        bias = jnp.concatenate([jnp.zeros((Q_BLOCK, L), jnp.float32),
                                jnp.where(valid, 0.0, NEG_INF).astype(jnp.float32)], axis=1)
        kk = jnp.concatenate([k_ctx, kbb], axis=1)
        vv = jnp.concatenate([v_ctx, vbb], axis=1)
        return _attend(qb, kk, vv, scale, bias=bias, sink=sink)

    qg = q.reshape(B, T, n_kv, H // n_kv, d)
    out = lax.map(blk, (_to_blocks(qg), kb, vb, jnp.arange(nb)))
    return _from_blocks(out).reshape(B, T, H * v_lat.shape[-1])

def _diff_dense(q, k, v, lam, scale):
    def blk(qb):
        s = jnp.einsum('bqhid,bkhid->bhiqk', qb, k).astype(jnp.float32) * scale
        p = jax.nn.softmax(s, axis=-1)
        p = p[:, :, 0] - lam * p[:, :, 1]
        return jnp.einsum('bhqk,bkhd->bqhd', p.astype(v.dtype), v)
    return _from_blocks(lax.map(blk, _to_blocks(q)))

def _mla_kv(ckv, kr, w_kvb, kn_g):
    B, L, _ = ckv.shape
    kv = (ckv @ w_kvb).reshape(B, L, D_HEADS, D_NOPE + D_V)
    k = jnp.concatenate([kv[..., :D_NOPE],
                         jnp.broadcast_to(kr[:, :, None, :], (B, L, D_HEADS, D_ROPE))], axis=-1)
    return _rms(k, kn_g), kv[..., D_NOPE:]

def _peer(h, wq, subkeys, u_tab, v_tab):
    B, T, D = h.shape
    n = B * T
    x = h.reshape(n, D)
    q = (x @ wq).reshape(n, PEER_HEADS, 2, PEER_HALF)
    s = jnp.einsum('nhpd,hpkd->nhpk', q, subkeys).astype(jnp.float32)
    sv, si = lax.top_k(s, PEER_TOPK)
    cand = (sv[:, :, 0, :, None] + sv[:, :, 1, None, :]).reshape(n, PEER_HEADS, PEER_TOPK * PEER_TOPK)
    cv, ci = lax.top_k(cand, PEER_TOPK)
    e1 = jnp.take_along_axis(si[:, :, 0, :], ci // PEER_TOPK, axis=-1)
    e2 = jnp.take_along_axis(si[:, :, 1, :], ci % PEER_TOPK, axis=-1)
    experts = (e1 * PEER_KEYS + e2).reshape(n // PEER_CHUNK, PEER_CHUNK, PEER_HEADS * PEER_TOPK)
    gates = jax.nn.softmax(cv, axis=-1).astype(h.dtype).reshape(n // PEER_CHUNK, PEER_CHUNK, PEER_HEADS * PEER_TOPK)
    xb = x.reshape(n // PEER_CHUNK, PEER_CHUNK, D)

    def blk(args):
        xc, ec, gc = args
        u = jnp.take(u_tab, ec, axis=0)
        a = jax.nn.gelu(jnp.einsum('cd,ckd->ck', xc, u), approximate=False)
        v = jnp.take(v_tab, ec, axis=0)
        return jnp.einsum('ck,ckd->cd', gc * a, v)

    return lax.map(blk, (xb, experts, gates)).reshape(B, T, D)

def _layer(x, mod, ctx, p, lam_init):
    is_ctx = ctx is None
    B, T, _ = x.shape
    sh1, sc1, g1, sh2, sc2, g2 = jnp.split(mod, 6, axis=-1)
    h = _rms(x, p['norm1_g']) * (1 + sc1) + sh1
    aq, ak, av, bq, bk, bv, cq, ck, cv, dqa, dckv, dkr, gates = _split_in(h @ p['w_in'])
    pos = (lambda t: t) if is_ctx else _axial_rope

    aq = pos(_rms(aq.reshape(B, T, A_HEADS, 2, A_QK), p['a_qk_g'][0]))
    ak = pos(_rms(ak.reshape(B, T, A_HEADS, 2, A_QK), p['a_qk_g'][1]))
    av = av.reshape(B, T, A_HEADS, A_V)
    lp = p['a_lam'].astype(jnp.float32)
    lam = jnp.exp(jnp.sum(lp[0] * lp[1])) - jnp.exp(jnp.sum(lp[2] * lp[3])) + lam_init
    ka = ak if is_ctx else jnp.concatenate([ctx['a_k'], ak], axis=1)
    va = av if is_ctx else jnp.concatenate([ctx['a_v'], av], axis=1)
    oa = _rms(_diff_dense(aq, ka, va, lam, A_QK ** -0.5), p['a_subln_g']) * (1.0 - lam_init)
    oa = oa.reshape(B, T, A_HEADS * A_V)

    bq = pos(_rms(bq.reshape(B, T, B_HEADS, HEAD_DIM), p['b_qk_g'][0]))
    bk = pos(_rms(bk.reshape(B, T, B_KV, HEAD_DIM), p['b_qk_g'][1]))
    bv = bv.reshape(B, T, B_KV, HEAD_DIM)
    sink = p['b_sink'].reshape(B_KV, B_HEADS // B_KV)
    if is_ctx:
        ob = _dense_gqa(bq, bk, bv, HEAD_DIM ** -0.5, sink)
    else:
        ob = _window_gqa(bq, bk, bv, ctx['b_k'], ctx['b_v'], HEAD_DIM ** -0.5, sink)

    cq = pos(_rms(cq.reshape(B, T, C_HEADS, HEAD_DIM), p['c_qk_g'][0]))
    ck = pos(_rms(ck.reshape(B, T, C_KV, HEAD_DIM), p['c_qk_g'][1]))
    cv = cv.reshape(B, T, C_KV, HEAD_DIM)
    kc = ck if is_ctx else jnp.concatenate([ctx['c_k'], ck], axis=1)
    vc = cv if is_ctx else jnp.concatenate([ctx['c_v'], cv], axis=1)
    oc = _dense_gqa(cq, kc, vc, HEAD_DIM ** -0.5)

    dq = (_rms(dqa, p['d_qnorm_g']) @ p['w_d_qb']).reshape(B, T, D_HEADS, D_QK)
    dq = _rms(dq, p['d_qk_g'][0])
    dckv = _rms(dckv, p['d_kvnorm_g'])
    kd, vd = _mla_kv(dckv, dkr, p['w_d_kvb'], p['d_qk_g'][1])
    if not is_ctx:
        dq = jnp.concatenate([dq[..., :D_NOPE], _axial_rope(dq[..., D_NOPE:])], axis=-1)
        kd = jnp.concatenate([kd[..., :D_NOPE], _axial_rope(kd[..., D_NOPE:])], axis=-1)
        kx, vx = _mla_kv(ctx['d_ckv'], ctx['d_krope'], p['w_d_kvb'], p['d_qk_g'][1])
        kd = jnp.concatenate([kx, kd], axis=1)
        vd = jnp.concatenate([vx, vd], axis=1)
    od = _dense_gqa(dq, kd, vd, D_QK ** -0.5)

    outs = jnp.stack([oa, ob, oc, od], axis=2)
    br = jnp.einsum('btie,ied->btid', outs, p['w_branch'])
    gt = jax.nn.sigmoid(gates.reshape(B, T, N_BRANCH, D_MODEL))
    y = jnp.sum(gt * br, axis=2) @ p['w_out']
    x = x + g1 * y

    h2 = _rms(x, p['norm2_g']) * (1 + sc2) + sh2
    x = x + g2 * _peer(h2, p['peer_wq'], p['peer_subkeys'], p['peer_u'], p['peer_v'])
    state = (ak, av, bk, bv, ck, cv, dckv, dkr) if is_ctx else None
    return x, state

def setup_inputs(seed: int = 0) -> dict:
    key = jax.random.key(seed)
    ks = iter(jax.random.split(key, 48))

    def nrm(shape, scale=1.0):
        return jax.random.normal(next(ks), shape, jnp.float32) * scale

    def gain(shape):
        return 1.0 + nrm(shape, 0.01)

    return {
        'x_prompt': nrm((BATCH, SEQ, D_MODEL)),
        'x_sample': nrm((DEC_BATCH, DEC_SEQ, D_MODEL)),
        'c': nrm((DEC_BATCH, D_MODEL)),
        'cache_a_k': nrm((DEC_BATCH, DEPTH, PAST_LEN, A_HEADS, 2, A_QK)),
        'cache_a_v': nrm((DEC_BATCH, DEPTH, PAST_LEN, A_HEADS, A_V)),
        'cache_b_k': nrm((DEC_BATCH, DEPTH, PAST_LEN, B_KV, HEAD_DIM)),
        'cache_b_v': nrm((DEC_BATCH, DEPTH, PAST_LEN, B_KV, HEAD_DIM)),
        'cache_c_k': nrm((DEC_BATCH, DEPTH, PAST_LEN, C_KV, HEAD_DIM)),
        'cache_c_v': nrm((DEC_BATCH, DEPTH, PAST_LEN, C_KV, HEAD_DIM)),
        'cache_d_ckv': nrm((DEC_BATCH, DEPTH, PAST_LEN, D_KV_LORA)),
        'cache_d_krope': nrm((DEC_BATCH, DEPTH, PAST_LEN, D_ROPE)),
        'c_ctx': nrm((D_MODEL,)),
        'ada_w': nrm((DEPTH, D_MODEL, 6 * D_MODEL), 0.5 * D_MODEL ** -0.5),
        'ada_b': nrm((DEPTH, 6 * D_MODEL), 0.01),
        'norm1_g': gain((DEPTH, D_MODEL)),
        'norm2_g': gain((DEPTH, D_MODEL)),
        'w_in': nrm((DEPTH, D_MODEL, IN_COLS), D_MODEL ** -0.5),
        'a_lam': nrm((DEPTH, 4, A_QK), 0.1),
        'a_qk_g': gain((DEPTH, 2, A_QK)),
        'a_subln_g': gain((DEPTH, A_V)),
        'b_sink': nrm((DEPTH, B_HEADS)),
        'b_qk_g': gain((DEPTH, 2, HEAD_DIM)),
        'c_qk_g': gain((DEPTH, 2, HEAD_DIM)),
        'd_qnorm_g': gain((DEPTH, D_Q_LORA)),
        'd_kvnorm_g': gain((DEPTH, D_KV_LORA)),
        'w_d_qb': nrm((DEPTH, D_Q_LORA, D_HEADS * D_QK), D_Q_LORA ** -0.5),
        'w_d_kvb': nrm((DEPTH, D_KV_LORA, D_HEADS * (D_NOPE + D_V)), D_KV_LORA ** -0.5),
        'd_qk_g': gain((DEPTH, 2, D_QK)),
        'w_branch': nrm((DEPTH, N_BRANCH, BRANCH_W, D_MODEL), BRANCH_W ** -0.5),
        'w_out': nrm((DEPTH, D_MODEL, D_MODEL), D_MODEL ** -0.5),
        'peer_wq': nrm((DEPTH, D_MODEL, PEER_HEADS * PEER_QDIM), D_MODEL ** -0.5),
        'peer_subkeys': nrm((DEPTH, PEER_HEADS, 2, PEER_KEYS, PEER_HALF), PEER_HALF ** -0.5),
        'peer_u': nrm((DEPTH, PEER_EXPERTS, D_MODEL), D_MODEL ** -0.5),
        'peer_v': nrm((DEPTH, PEER_EXPERTS, D_MODEL), PEER_HEADS ** -0.5),
    }

def reference(x_prompt, x_sample, c, cache_a_k, cache_a_v, cache_b_k, cache_b_v, cache_c_k, cache_c_v,
              cache_d_ckv, cache_d_krope, c_ctx, ada_w, ada_b, norm1_g, norm2_g, w_in, a_lam, a_qk_g,
              a_subln_g, b_sink, b_qk_g, c_qk_g, d_qnorm_g, d_kvnorm_g, w_d_qb, w_d_kvb, d_qk_g,
              w_branch, w_out, peer_wq, peer_subkeys, peer_u, peer_v):
    y_prompt = x_prompt
    y_sample = x_sample
    states = [[] for _ in range(8)]
    for l in range(DEPTH):
        p = {'norm1_g': norm1_g[l], 'norm2_g': norm2_g[l], 'w_in': w_in[l], 'a_lam': a_lam[l],
             'a_qk_g': a_qk_g[l], 'a_subln_g': a_subln_g[l], 'b_sink': b_sink[l], 'b_qk_g': b_qk_g[l],
             'c_qk_g': c_qk_g[l], 'd_qnorm_g': d_qnorm_g[l], 'd_kvnorm_g': d_kvnorm_g[l],
             'w_d_qb': w_d_qb[l], 'w_d_kvb': w_d_kvb[l], 'd_qk_g': d_qk_g[l], 'w_branch': w_branch[l],
             'w_out': w_out[l], 'peer_wq': peer_wq[l], 'peer_subkeys': peer_subkeys[l],
             'peer_u': peer_u[l], 'peer_v': peer_v[l]}
        lam_init = 0.8 - 0.6 * math.exp(-0.3 * l)
        mod_ctx = (jax.nn.silu(c_ctx) @ ada_w[l] + ada_b[l])[None, None, :]
        y_prompt, st = _layer(y_prompt, mod_ctx, None, p, lam_init)
        for lst, s in zip(states, st):
            lst.append(s)
        ctx = {'a_k': cache_a_k[:, l], 'a_v': cache_a_v[:, l], 'b_k': cache_b_k[:, l], 'b_v': cache_b_v[:, l],
               'c_k': cache_c_k[:, l], 'c_v': cache_c_v[:, l], 'd_ckv': cache_d_ckv[:, l],
               'd_krope': cache_d_krope[:, l]}
        mod_lat = (jax.nn.silu(c) @ ada_w[l] + ada_b[l])[:, None, :]
        y_sample, _ = _layer(y_sample, mod_lat, ctx, p, lam_init)
    new_a_k = jnp.stack(states[0], axis=1)
    new_a_v = jnp.stack(states[1], axis=1)
    new_b_k = jnp.stack(states[2], axis=1)
    new_b_v = jnp.stack(states[3], axis=1)
    new_c_k = jnp.stack(states[4], axis=1)
    new_c_v = jnp.stack(states[5], axis=1)
    new_d_ckv = jnp.stack(states[6], axis=1)
    new_d_krope = jnp.stack(states[7], axis=1)
    return (y_prompt, y_sample, new_a_k, new_a_v, new_b_k, new_b_v, new_c_k, new_c_v, new_d_ckv, new_d_krope)


_drawn_inputs = setup_inputs


def setup_inputs(seed=0):
    import zlib

    import numpy as np

    out = dict(_drawn_inputs(seed))
    spreads = {}
    factors = {'cache_b_k': 4.177,
     'cache_b_v': 3.544,
     'cache_c_k': 6.351,
     'cache_c_v': 5.279,
     'cache_d_ckv': 5.578,
     'cache_d_krope': 8.0,
     'ada_b': 3.677,
     'norm1_g': 5.673,
     'norm2_g': 6.294,
     'a_lam': 8.0,
     'a_qk_g': 6.358,
     'a_subln_g': 8.0,
     'b_sink': 8.0,
     'b_qk_g': 5.537,
     'c_qk_g': 6.255,
     'd_qnorm_g': 8.0,
     'd_kvnorm_g': 5.326,
     'd_qk_g': 8.0}
    for name, (base, spread) in spreads.items():
        noise = np.random.default_rng([zlib.crc32(name.encode()), seed]).standard_normal(out[name].shape)
        drawn = base * np.exp(spread * noise) if base else spread * noise
        out[name] = jnp.asarray(drawn.astype(out[name].dtype))
    for name, factor in factors.items():
        out[name] = (out[name] * factor).astype(out[name].dtype)
    return out
```

```python
import math
from contextlib import ExitStack

import numpy as np

import concourse.bass as bass
from concourse import mybir

F32 = mybir.dt.float32
U32 = mybir.dt.uint32
ALU = mybir.AluOpType
ACT = mybir.ActivationFunctionType
AX = mybir.AxisListType

P = 128
D = 1024
DC = D // P
DEPTH = 2
LAT, CTX, PAST = 512, 128, 128
TOK = LAT + CTX
KEYS = LAT + PAST + CTX
NEWK = LAT + PAST
TILES = TOK // P
KTILES = KEYS // P
EPS = 1e-6
NEG = -1e30
LOWEST = -3.0e38

A_QK, HD, D_QK, D_NOPE, D_ROPE = 32, 64, 96, 64, 32
HEADS = 4
SCALE = {"A": A_QK ** -0.5, "B": HD ** -0.5, "C": HD ** -0.5, "D": D_QK ** -0.5}

PH, PK, TOPK = 8, 128, 16
SUB = 2 * PH
E1 = PK

RING = 4
SLOT = 1280
N_ADA, N_FM, N_V, N_GATE, N_WOUT, N_WQ = 48, 14, 4, 32, 8, 16
B_FM = N_ADA
B_V = B_FM + N_FM
B_DQ = B_V + N_V
B_KV = B_DQ + 1
B_GATE = B_KV + 1
B_WOUT = B_GATE + N_GATE
B_WQ = B_WOUT + N_WOUT
BLOCKS = B_WQ + N_WQ
assert BLOCKS % RING == 0 and B_GATE % RING == 0
PER_SLOT = BLOCKS // RING

G_ADAB, G_N1, G_N2 = 0, 96, 112
G_AQ, G_AK, G_BQ, G_BK, G_CQ, G_CK = range(128, 134)
G_QA, G_CKV, G_DQ, G_DK, G_SUB = 134, 136, 137, 138, 139
G_LAM, G_SINK, G_LINIT, G_LREST = 140, 268, 272, 273
G_ALL = 274

C_ONES, C_G32, C_G64, C_RA, C_RB, C_RD, C_ID, C_PREV, C_NEXT, C_IOTA, C_SEL = [P * i for i in range(11)]
C_I16 = P * 11
C_EPS = C_I16 + 16
C_ALL = C_EPS + 1
TRIG = 6 * LAT


class Arena:

    def __init__(self, tensor, start, size):
        self.tensor, self.at, self.end = tensor, start, size

    def take(self, *dims):
        n = int(np.prod(dims))
        ap = self.tensor[:, self.at:self.at + n]
        self.at += n
        assert self.at <= self.end, (self.at, self.end)
        if len(dims) == 2:
            ap = ap.rearrange("p (a b) -> p a b", a=dims[0])
        if len(dims) == 3:
            ap = ap.rearrange("p (a b c) -> p a b c", a=dims[0], b=dims[1])
        return ap


def build(nc, xT, csT, consts, trig, vecs, ada, wfm, wv, wdq, wkv, wgate, wout, wq, subk, uT, vtab,
          cache_k, cache_kr, cache_v, yT, st_k, st_kr, st_v):
    gates = nc.dram_tensor("gates_by_expert", (E1, P, TOK), F32, kind="Internal").ap()

    items = ([("aq", 0), ("aq", 1), ("ak", 0), ("ak", 1), ("bq", 0), ("bq", 1), ("bk", 0), ("cq", 0), ("cq", 1),
              ("ck", 0), ("qa", 0), ("qa", 1), ("ckv", 0), ("kr", 0)]
             + [("dq", h) for h in range(HEADS)] + [("dk", h) for h in range(HEADS)])
    NI = len(items)
    ROPED = {"aq", "ak", "bq", "bk", "cq", "ck", "dq", "dk"}
    norm_no = {n: i for i, n in enumerate(n for n in range(NI) if items[n] not in (("qa", 0), ("kr", 0)))}
    rope_no = {n: i for i, n in enumerate(n for n in range(NI) if items[n][0] in ROPED)}
    NN, NR = len(norm_no), len(rope_no)
    at_item = {it: n for n, it in enumerate(items)}

    units = [(br, j, t, hh) for br in "ABCD" for j in range(2) for t in range(TILES) for hh in range(2)]
    maps = [(u, m) for u, x in enumerate(units) for m in range(2 if x[0] == "A" else 1)]
    maps_of = [[g for g, (uu, _) in enumerate(maps) if uu == u] for u in range(len(units))]
    NU, NM = len(units), len(maps)
    NBAR = 8

    with ExitStack() as ctx:
        def sb(name, shape, dt=F32):
            return ctx.enter_context(nc.sbuf_tensor(name, shape, dt))

        def sem(name):
            return ctx.enter_context(nc.semaphore(name))

        XT = sb("XT", [P, DC, TOK])
        HT = sb("HT", [P, DC, TOK])
        WR = sb("WR", [P, RING, SLOT])
        CN = sb("CN", [P, C_ALL])
        GN = sb("GN", [P, G_ALL])
        MD = sb("MD", [P, 96])
        CS = sb("CS", [P, 16])
        SM = sb("SM", [P, 160])
        IDLE = sb("IDLE", [P, 64])
        AF = 37500
        AR = sb("AR", [P, AF])
        PS = ctx.enter_context(nc.psum_tensor("PS", [P, 8, 512], F32))
        PF = PS[:, :, :].rearrange("p a b -> p (a b)")

        def bank(b, n=512, parts=P):
            return PF[0:parts, 512 * b:512 * b + n]

        ones, grp32, grp64 = (CN[:, c:c + P] for c in (C_ONES, C_G32, C_G64))
        rot32, rot64 = CN[:, C_RA:C_RA + P], CN[:, C_RB:C_RB + P]
        rot96 = CN[0:D_QK, C_RD:C_RD + D_QK]
        ident = CN[:, C_ID:C_ID + P]
        band = {"prev": CN[:, C_PREV:C_PREV + P], "next": CN[:, C_NEXT:C_NEXT + P]}
        iota = CN[:, C_IOTA:C_IOTA + P]
        sel_kr = CN[0:D_ROPE, C_SEL:C_SEL + D_QK]
        iota16 = CN[:, C_I16:C_I16 + 16]
        eps = CN[:, C_EPS:C_EPS + 1]
        MD4 = MD[:, :].rearrange("p (w c g) -> p w c g", w=6, c=DC)
        SC = SM[:, 0:32].rearrange("p (n c g) -> p n c g", n=2, c=DC)
        LAMP, LAMS, LAME, NLAM, GSUB = SM[:, 32:96], SM[:, 96:98], SM[:, 98:100], SM[:, 100:101], SM[:, 101:102]
        MX, NM_, SU, RC, ES = (SM[:, 104 + 8 * i:112 + 8 * i] for i in range(5))

        a = Arena(AR, 0, AF)
        KT = a.take(5, KEYS)
        KR = a.take(KEYS)
        DK = a.take(HEADS, KEYS)
        QT = a.take(6, TOK)
        DQ = a.take(HEADS, TOK)
        QA = a.take(2, TOK)
        VT = a.take(KTILES, 512)
        VD = a.take(KTILES, 256)
        shared = a.at
        q_ = Arena(AR, shared, AF)
        TG = q_.take(6, LAT)
        YB, SQ, YN = q_.take(2, KEYS), q_.take(2, KEYS), q_.take(2, LAT)
        STD, RST = q_.take(2, KEYS), q_.take(KEYS)
        SQX, T1, T2 = q_.take(TOK), q_.take(2, LAT), q_.take(LAT)
        t_ = Arena(AR, shared, AF)
        OUT = t_.take(8, TOK)
        heads_end = t_.at
        PB = t_.take(3, 2, 640)
        PT = t_.take(2, 640)
        u_ = Arena(AR, heads_end, AF)
        HSQ, HSTD, HRS = u_.take(2, TOK), u_.take(2, TOK), u_.take(2, TOK)
        g_ = Arena(AR, 0, shared)
        YS, SG, GM = g_.take(DC, TOK), g_.take(2, TOK), g_.take(2, TOK)
        n_ = Arena(AR, 0, AF)
        NSQ, NSTD, NRS = n_.take(DC, TOK), n_.take(TOK), n_.take(TOK)
        p_ = Arena(AR, 0, AF)
        PQ, SK = p_.take(SUB, TOK), p_.take(SUB, PK)
        V1, I1, I1F = p_.take(SUB, TOPK), p_.take(SUB, TOPK), p_.take(SUB, TOPK)
        CV, CI, CM, CE = p_.take(PH, TOPK), p_.take(PH, TOPK), p_.take(PH, TOPK), p_.take(PH, TOPK)
        CA, CB, CAF, CBF = p_.take(PH, TOPK), p_.take(PH, TOPK), p_.take(PH, TOPK), p_.take(PH, TOPK)
        EW = p_.take(3, P)
        EWT = p_.take(3, P)
        CSUM, CRC = p_.take(PH), p_.take(PH)
        HOT = p_.take(2, 8, P)
        GB = p_.take(P, P)
        S1, S2 = p_.take(SUB * PK), p_.take(SUB * PK)
        d_ = Arena(AR, 0, AF)
        UB, VB, GT, HB, AC = d_.take(4, D), d_.take(8, D), d_.take(8, TOK), d_.take(8, TOK), d_.take(DC, TOK)

        bar, layer_free = sem("phase_ends"), sem("layer_free")
        c_in, l_in, x_in = sem("consts_in"), sem("layer_in"), sem("x_in")
        w_in = [sem(f"weights_in{k}") for k in range(RING)]
        w_used = sem("weights_used")
        cs_ready, mod_copied, lam_sum, lam_exp = sem("cs_ready"), sem("mod_copied"), sem("lam_sum"), sem("lam_exp")
        cs_sig = sem("cs_sig")
        sq_ready, ss_ready, std_ready = sem("norm_squares"), sem("norm_sums"), sem("norm_std")
        pj_ready, y_ready, qs_ready, qstd_ready = sem("proj_ready"), sem("raw_ready"), sem("head_sums"), sem("head_std")
        yn_ready, rot_ready, t1_ready, rope_done = sem("normed"), sem("rotated"), sem("cos_part"), sem("rope_done")
        v_out = sem("v_out")
        st_out = sem("states_out")
        s_ready, nm_ready, exp_done, p_ready = sem("scores"), sem("neg_max"), sem("exp_done"), sem("probs")
        t_ready, pt_ready, pv_done, o_done = sem("probs_turned"), sem("probs_t_out"), sem("pv_done"), sem("heads_out")
        sub_sq, sub_ss, sub_std = sem("sub_squares"), sem("sub_sums"), sem("sub_std")
        g_ready, sg_ready, gm_free = sem("gate_ready"), sem("sigmoid_ready"), sem("gated")
        wo_done, q_done = sem("residual_added"), sem("peer_q_out")
        sc_ready, s_evac, cm_ready, ce_ready, tk_ready = (sem(n) for n in (
            "sub_scores", "sub_scores_out", "chosen_minus_max", "chosen_exp", "choice_ready"))
        tr_ready, ewt_ready, hot_ready, gmm_done, g_evac, gd_out = (sem(n) for n in (
            "choice_turned", "choice_t_out", "one_hots", "gates_spread", "gates_copied", "gates_stored"))
        u_in = [sem(f"u_in{k}") for k in range(4)]
        v_in, g_in = [sem(f"v_in{k}") for k in range(2)], [sem(f"g_in{k}") for k in range(2)]
        u_used, ge_done, h_ready, o_ready, ac_done = (sem(n) for n in (
            "u_used", "gelu_done", "gated_gelu", "expert_sums", "expert_sums_added"))
        y_out = sem("y_out")

        idle_cells = iter(range(64))

        def settled(eng):
            n = next(idle_cells)
            cell = IDLE[:, n:n + 1]
            if eng.engine == nc.vector.engine:
                nc.vector.memset(cell, 0.0)
            elif eng.engine == nc.scalar.engine:
                nc.scalar.copy(cell, eps)
            elif eng.engine == nc.gpsimd.engine:
                nc.gpsimd.tensor_tensor(cell, eps, eps, ALU.mult)
            else:
                nc.tensor.matmul(bank(7)[:, 508:510], ident, iota[:, 0:2], start=True, stop=True)

        def phase_end(eng, l, n):
            eng.drain().then_inc(bar, 1)
            eng.wait_ge(bar, l * (4 * NBAR) + 4 * (n + 1))
            settled(eng)

        def qcols(t):
            return slice(P * t, P * t + P)

        block = ctx.enter_context(nc.Block())

        @block.sync
        def _(sp):
            sp.dma_start(CN[:, :], consts).then_inc(c_in, 16)
            sp.dma_start(CS[:, :], csT).then_inc(c_in, 16)
            sp.dma_start(XT[:, :, :], xT).then_inc(x_in, 16)

            def load(l, n, dst, src):
                sp.wait_ge(w_used, l * BLOCKS + (n + 1))
                sp.dma_start(dst, src).then_inc(w_in[n % RING], 16)

            with sp.Fori(0, DEPTH) as l:
                sp.wait_ge(layer_free, l + 1)
                sp.dma_start(GN[:, :], vecs[l]).then_inc(l_in, 16)
                with sp.Fori(0, N_ADA // RING) as i:
                    for k in range(RING):
                        sp.wait_ge(w_used, l * BLOCKS + i * RING + (k + 1))
                        sp.dma_start(WR[:, k, 0:D], ada[l, i * RING + k]).then_inc(w_in[k], 16)
                sp.wait_ge(bar, l * (4 * NBAR) + 4)
                sp.dma_start(TG[:, :, :], trig).then_inc(l_in, 16)
                sp.dma_start(KT[:, :, LAT:NEWK], cache_k[l]).then_inc(l_in, 16)
                sp.dma_start(KR[0:D_ROPE, LAT:NEWK], cache_kr[l]).then_inc(l_in, 16)
                sp.dma_start(VT[:, 4, :], cache_v[l]).then_inc(l_in, 16)
                for n in range(N_FM):
                    load(l, B_FM + n, WR[:, (B_FM + n) % RING, 0:D], wfm[l, n])
                for n in range(N_V):
                    load(l, B_V + n, WR[:, (B_V + n) % RING, 0:D], wv[l, n])
                load(l, B_DQ, WR[:, B_DQ % RING, 0:2 * HEADS * D_QK], wdq[l])
                load(l, B_KV, WR[:, B_KV % RING, 0:HEADS * (D_QK + HD)], wkv[l])
                with sp.Fori(0, N_GATE // RING) as i:
                    for k in range(RING):
                        sp.wait_ge(w_used, l * BLOCKS + i * RING + (B_GATE + k + 1))
                        sp.dma_start(WR[:, k, 0:SLOT], wgate[l, i * RING + k]).then_inc(w_in[k], 16)
                for n in range(N_WOUT):
                    load(l, B_WOUT + n, WR[:, (B_WOUT + n) % RING, 0:D], wout[l, n])
                for n in range(N_WQ):
                    if n == RING:
                        sp.wait_ge(bar, l * (4 * NBAR) + 4 * 6)
                        sp.dma_start(SK[:, :, :], subk[l]).then_inc(l_in, 16)
                    load(l, B_WQ + n, WR[:, (B_WQ + n) % RING, 0:D], wq[l, n])
                for t in range(TILES):
                    sp.wait_ge(g_evac, l * (32 * TILES) + 32 * (t + 1) + 2)
                    sp.dma_start(gates[:, :, qcols(t)].rearrange("a b t -> b a t"), GB[:, :, :]).then_inc(gd_out, 16)
                with sp.Fori(0, E1 // 8) as i:
                    for half in range(2):
                        for k in range(4):
                            if half == 0 and k == 0:
                                sp.wait_ge(bar, l * (4 * NBAR) + 4 * 7)
                                sp.wait_ge(gd_out, l * (16 * TILES) + 16 * TILES)
                            sp.wait_ge(u_used, l * E1 + i * 8 + (4 * half + k + 1))
                            sp.dma_start(UB[:, k, :], uT[l, i * 8 + (4 * half + k)]).then_inc(u_in[k], 16)
                            if k == 0:
                                sp.wait_ge(o_ready, l * 256 + i * 16 + (8 * half + 8))
                                sp.dma_start(GT[:, 4 * half:4 * half + 4, :],
                                             gates[bass.ds(i * 8 + 4 * half, 4)].rearrange("a b t -> b a t")
                                             ).then_inc(g_in[half], 16)
                                sp.dma_start(VB[:, 4 * half:4 * half + 4, :],
                                             vtab[l, bass.ds(i * 8 + 4 * half, 4)].rearrange("a b d -> b a d")
                                             ).then_inc(v_in[half], 16)
            sp.wait_ge(layer_free, DEPTH + 1)
            sp.dma_start(yT, XT[:, :, :]).then_inc(y_out, 16)
            sp.wait_ge(y_out, 16)
            sp.wait_ge(st_out, 48 * DEPTH)

        @block.tensor
        def _(pe):
            for _ in range(RING):
                pe.nop().then_inc(w_used, 1)
            for _ in range(4):
                pe.nop().then_inc(u_used, 1)
            for _ in range(16):
                pe.nop().then_inc(o_ready, 1)
            for _ in range(2):
                pe.nop().then_inc(gmm_done, 1)

            def both(out, lhsT, rhs, start, stop, n=TOK):
                pe.matmul(out(0, 512), lhsT, rhs(0, 512), start=start, stop=stop)
                return pe.matmul(out(512, n), lhsT, rhs(512, n), start=start, stop=stop)

            def cols(base, parts=P):
                return lambda lo, hi: PF[0:parts, base + lo:base + hi]

            def weights(l, n):
                pe.wait_ge(w_in[n % RING], l * (16 * PER_SLOT) + 16 * (n // RING + 1))
                return WR[:, n % RING, :]

            def norm(l, which):
                for c in range(DC):
                    pe.wait_ge(sq_ready, l * (2 * DC) + (which * DC + c + 1))
                    last = both(cols(0), ones, lambda lo, hi: NSQ[:, c, lo:hi], c == 0, c == DC - 1)
                last.then_inc(ss_ready, 1)

            def project(l, n):
                kind, j = items[n]
                base = 1024 * (n % 2)
                if n >= 2:
                    pe.wait_ge(y_ready, l * NI + (n - 1))
                if kind == "dq":
                    w = weights(l, B_DQ)
                    if j == 0:
                        pe.wait_ge(yn_ready, l * NN + (norm_no[at_item["qa", 1]] + 1))
                        pe.wait_ge(v_out, (l + 1) * TILES)
                    for kc in range(2):
                        lhsT = w[:, kc * HEADS * D_QK + j * D_QK:kc * HEADS * D_QK + (j + 1) * D_QK]
                        last = both(cols(base, D_QK), lhsT, lambda lo, hi: QA[:, kc, lo:hi], kc == 0, kc == 1)
                    last.then_inc(w_used if j == HEADS - 1 else pj_ready, 1)
                elif kind == "dk":
                    w = weights(l, B_KV)
                    both(cols(base, D_QK), w[:, j * D_QK:(j + 1) * D_QK], lambda lo, hi: KT[:, 4, lo:hi], True, False, KEYS)
                    both(cols(base, D_QK), sel_kr, lambda lo, hi: KR[0:D_ROPE, lo:hi], False, True, KEYS).then_inc(pj_ready, 1)
                else:
                    w = weights(l, B_FM + n)
                    for c in range(DC):
                        last = both(cols(base), w[:, c * P:(c + 1) * P], lambda lo, hi: HT[:, c, lo:hi], c == 0, c == DC - 1)
                    last.then_inc(w_used, 1)

            def head_sums(l, n):
                kind, _ = items[n]
                if n not in norm_no:
                    return
                pe.wait_ge(y_ready, l * NI + (n + 1))
                if norm_no[n] >= 1:
                    pe.wait_ge(qstd_ready, l * NN + norm_no[n])
                parts = D_QK if kind in ("dq", "dk") else P
                group = {"aq": grp32, "ak": grp32, "bq": grp64, "bk": grp64, "cq": grp64, "ck": grp64,
                         "qa": ones, "ckv": ones}.get(kind, CN[0:D_QK, C_ONES:C_ONES + D_QK])
                if kind == "qa":
                    both(cols(2048), ones, lambda lo, hi: SQX[:, lo:hi], True, False)
                both(cols(2048, parts), group, lambda lo, hi: SQ[0:parts, n % 2, lo:hi], kind != "qa", True,
                     KEYS if kind == "dk" else TOK).then_inc(qs_ready, 1)

            def rotate(l, n):
                if n not in rope_no:
                    return
                kind, _ = items[n]
                r = rope_no[n]
                pe.wait_ge(yn_ready, l * NN + (norm_no[n] + 1))
                if r >= 1:
                    pe.wait_ge(rope_done, l * NR + r)
                parts = D_QK if kind in ("dq", "dk") else P
                m = rot32 if kind[0] == "a" else rot96 if kind[0] == "d" else rot64
                pe.matmul(bank(6, LAT, parts), m, YN[0:parts, r % 2, :], start=True, stop=True).then_inc(rot_ready, 1)

            def values(l):
                pe.wait_ge(y_ready, l * NI + N_FM)
                for n in range(N_V):
                    w = weights(l, B_V + n)
                    for t in range(TILES):
                        for cc in range(2):
                            c = 2 * n + cc
                            last = pe.matmul(bank(t if t < 4 else 7), HT[:, c, qcols(t)], w[:, cc * 512:(cc + 1) * 512],
                                             start=c == 0, stop=c == DC - 1)
                    last.then_inc(w_used, 1)

            def d_values(l):
                pe.wait_ge(y_ready, l * NI + NI)
                w = weights(l, B_KV)
                for t in range(KTILES):
                    last = pe.matmul(PF[:, 256 * t:256 * t + 256], KT[:, 4, qcols(t)], w[:, HEADS * D_QK:HEADS * (D_QK + HD)],
                                     start=True, stop=True)
                last.then_inc(w_used, 1)

            def scores(l, u):
                br, j, t, hh = units[u]
                h = 2 * j + hh
                for g in maps_of[u]:
                    if g >= 2:
                        pe.wait_ge(exp_done, l * NM + (g - 1))
                    if br == "A":
                        f = 2 * h + maps[g][1]
                        rows = slice(32 * (f % 4), 32 * (f % 4) + 32)
                        q, k = QT[rows, f // 4, qcols(t)], KT[rows, f // 4, :]
                    elif br == "D":
                        q, k = DQ[0:D_QK, h, qcols(t)], DK[0:D_QK, h, :]
                    else:
                        rows = slice(64 * (h // 2), 64 * (h // 2) + 64)
                        b = 2 if br == "B" else 4
                        q, k = QT[rows, b + h % 2, qcols(t)], KT[rows, 2 if br == "B" else 3, :]
                    at = 1024 * (g % 2)
                    for lo, hi in key_spans(br, t):
                        last = pe.matmul(PF[:, at:at + hi - lo], q, k[:, lo:hi], start=True, stop=True)
                        at += hi - lo
                    last.then_inc(s_ready, 1)

            def turn(l, u):
                br, j, t, hh = units[u]
                pe.wait_ge(p_ready, l * NU + (u + 1))
                if u >= 1:
                    pe.wait_ge(pt_ready, l * NU + u)
                for i in range(len(key_tiles(br, t))):
                    last = pe.transpose(PF[:, 2048 + P * i:2048 + P * i + P], PB[:, u % 3, 0, P * i:P * i + P], ident)
                last.then_inc(t_ready, 1)

            def weigh(l, u):
                br, j, t, hh = units[u]
                h = 2 * j + hh
                pe.wait_ge(pt_ready, l * NU + (u + 1))
                if hh == 0 and u >= 4:
                    pe.wait_ge(o_done, l * (NU // 2) + (u // 2 - 1))
                v = {"A": lambda kt: VT[:, kt, 64 * h:64 * h + 64],
                     "B": lambda kt: VT[:, kt, 256 + 64 * (h // 2):320 + 64 * (h // 2)],
                     "C": lambda kt: VT[:, kt, 384 + 64 * (h // 2):448 + 64 * (h // 2)],
                     "D": lambda kt: VD[:, kt, 64 * h:64 * h + 64]}[br]
                tiles = key_tiles(br, t)
                out = PF[64 * hh:64 * hh + 64, 3072 + 512 * (u // 2 % 2):3072 + 512 * (u // 2 % 2) + P]
                for i, kt in enumerate(tiles):
                    last = pe.matmul(out, v(kt), PT[:, u % 2, P * i:P * i + P], start=i == 0, stop=i == len(tiles) - 1)
                last.then_inc(pv_done, 1)

            pe.wait_ge(c_in, 32)
            pe.wait_ge(cs_ready, 1)
            with pe.Fori(0, DEPTH) as l:
                norm(l, 0)
                with pe.Fori(0, N_ADA // RING) as i:
                    for k in range(RING):
                        pe.wait_ge(w_in[k], l * (16 * PER_SLOT) + i * 16 + 16)
                        if k == 0:
                            pe.wait_ge(mod_copied, l * (N_ADA // RING) + i + 1)
                        for c in range(DC):
                            last = pe.matmul(bank(7, 8)[:, 2 * k:2 * k + 2], WR[:, k, c * P:(c + 1) * P], CS[:, 2 * c:2 * c + 2],
                                             start=c == 0, stop=c == DC - 1)
                        last.then_inc(w_used, 1)
                phase_end(pe, l, 0)
                pe.wait_ge(l_in, l * 96 + 80)
                for s in range(NI + 2):
                    if s == N_FM:
                        values(l)
                    if s < NI:
                        if items[s] == ("dk", 0):
                            pe.wait_ge(yn_ready, l * NN + (norm_no[at_item["ckv", 0]] + 1))
                        project(l, s)
                    if 1 <= s <= NI:
                        head_sums(l, s - 1)
                    if s >= 2:
                        rotate(l, s - 2)
                d_values(l)
                phase_end(pe, l, 1)
                for s in range(NU + 3):
                    if s < NU:
                        scores(l, s)
                    if 2 <= s < NU + 2:
                        turn(l, s - 2)
                    if s >= 3:
                        weigh(l, s - 3)
                phase_end(pe, l, 2)
                for j in range(2):
                    pe.wait_ge(sub_sq, l * 2 + (j + 1))
                    both(cols(1024 * j), grp64, lambda lo, hi: HSQ[:, j, lo:hi], True, True).then_inc(sub_ss, 1)
                phase_end(pe, l, 3)
                with pe.Fori(0, DC) as i:
                    for k in range(4):
                        pe.wait_ge(w_in[k], l * (16 * PER_SLOT) + i * 16 + 16 * (B_GATE // RING + 1))
                        pe.wait_ge(gm_free, l * N_GATE + i * 4 + (k + 1))
                        for c in range(DC):
                            last = both(cols(1024 * (k % 2)), WR[:, k, c * P:(c + 1) * P], lambda lo, hi: HT[:, c, lo:hi],
                                        c == 0, c == DC - 1)
                        last.then_inc(g_ready, 1)
                        for e in range(2):
                            last = both(cols(2048 + 1024 * (k % 2)), WR[:, k, D + e * P:D + (e + 1) * P],
                                        lambda lo, hi: OUT[:, 2 * k + e, lo:hi], e == 0, e == 1)
                        last.then_inc(w_used, 1)
                pe.wait_ge(gm_free, l * N_GATE + (N_GATE + 2))
                for n in range(N_WOUT):
                    w = weights(l, B_WOUT + n)
                    if n >= 2:
                        pe.wait_ge(wo_done, l * N_WOUT + (n - 1))
                    for c in range(DC):
                        last = both(cols(1024 * (n % 2)), w[:, c * P:(c + 1) * P], lambda lo, hi: YS[:, c, lo:hi],
                                    c == 0, c == DC - 1)
                    last.then_inc(w_used, 1)
                phase_end(pe, l, 4)
                norm(l, 1)
                phase_end(pe, l, 5)
                for n in range(N_WQ):
                    w = weights(l, B_WQ + n)
                    if n >= 4:
                        pe.wait_ge(q_done, l * N_WQ + (n - 3))
                    for c in range(DC):
                        last = both(cols(1024 * (n % 4)), w[:, c * P:(c + 1) * P], lambda lo, hi: HT[:, c, lo:hi],
                                    c == 0, c == DC - 1)
                    last.then_inc(w_used, 1)
                pe.wait_ge(q_done, l * N_WQ + N_WQ)
                pe.wait_ge(l_in, l * 96 + 96)

                def sub_scores(t):
                    if t >= 1:
                        pe.wait_ge(s_evac, l * TILES + t)
                    for b in range(SUB):
                        last = pe.matmul(PF[:, P * b:P * b + P], PQ[:, b, qcols(t)], SK[:, b, :], start=True, stop=True)
                    last.then_inc(sc_ready, 1)

                sub_scores(0)
                for t in range(TILES):
                    pe.wait_ge(tk_ready, l * TILES + (t + 1))
                    for i in range(3):
                        last = pe.transpose(PF[:, 2048 + P * i:2048 + P * i + P], EW[:, i, :], ident)
                    last.then_inc(tr_ready, 1)
                    if t + 1 < TILES:
                        sub_scores(t + 1)
                    with pe.Fori(0, 16) as i:
                        for b in range(2):
                            pe.wait_ge(hot_ready, l * (32 * TILES) + i * 2 + (32 * t + b + 1))
                            pe.wait_ge(g_evac, l * (32 * TILES) + i * 2 + (32 * t + b + 1))
                            for k in range(4):
                                last = pe.matmul(bank(5 + b)[:, P * k:P * k + P], HOT[:, b, 2 * k, :], HOT[:, b, 2 * k + 1, :],
                                                 start=True, stop=True)
                            last.then_inc(gmm_done, 1)
                phase_end(pe, l, 6)
                with pe.Fori(0, E1 // 8) as i:
                    for k in range(8):
                        pe.wait_ge(u_in[k % 4], l * (16 * E1 // 4) + i * 32 + (16 * (k // 4) + 16))
                        pe.wait_ge(ge_done, l * E1 + i * 8 + (k + 1))
                        for c in range(DC):
                            last = both(cols(1024 * (k % 2)), UB[:, k % 4, c * P:(c + 1) * P], lambda lo, hi: HT[:, c, lo:hi],
                                        c == 0, c == DC - 1)
                        last.then_inc(u_used, 1)
                    for half in range(2):
                        pe.wait_ge(v_in[half], l * (16 * E1 // 8) + i * 16 + 16)
                        pe.wait_ge(h_ready, l * E1 + i * 8 + (4 * half + 4))
                        for d in range(DC):
                            pe.wait_ge(ac_done, l * 256 + i * 16 + (8 * half + d + 1))
                            for k in range(4):
                                e = 4 * half + k
                                last = both(cols(2048 + 1024 * (d % 2)), VB[:, e, d * P:(d + 1) * P],
                                            lambda lo, hi: HB[:, e, lo:hi], k == 0, k == 3)
                            last.then_inc(o_ready, 1)
                phase_end(pe, l, 7)

        @block.scalar
        def _(act):
            for _ in range(2):
                act.nop().then_inc(ge_done, 1)
                act.nop().then_inc(g_evac, 1)
            act.wait_ge(c_in, 32)
            nc.scalar.activation(SM[:, 144:160], CS[:, :], ACT.Sigmoid).then_inc(cs_sig, 1)
            act.wait_ge(x_in, 16)

            def norm(l, which):
                for c in range(DC):
                    nc.scalar.activation(NSQ[:, c, :], XT[:, c, :], ACT.Square).then_inc(sq_ready, 1)
                act.wait_ge(ss_ready, l * 2 + (which + 1))
                nc.scalar.activation(NSTD, PF[:, 0:TOK], ACT.Sqrt, bias=eps, scale=1.0 / D).then_inc(std_ready, 1)

            def used(l, n):
                act.wait_ge(w_used, l * BLOCKS + (RING + n + 1))

            def raw(l, n):
                kind, j = items[n]
                base = 1024 * (n % 2)
                if n < N_FM or (kind, j) == ("dq", HEADS - 1):
                    used(l, B_FM + n if n < N_FM else B_DQ)
                else:
                    act.wait_ge(pj_ready, l * (2 * HEADS - 1) + (j + 1 if kind == "dq" else HEADS + j))
                if kind == "kr":
                    nc.scalar.copy(KR[0:D_ROPE, 0:LAT], PF[0:D_ROPE, base:base + LAT])
                    nc.scalar.copy(KR[0:D_ROPE, NEWK:KEYS], PF[0:D_ROPE, base + LAT:base + TOK]).then_inc(y_ready, 1)
                    return
                if (kind, j) == ("qa", 0):
                    nc.scalar.copy(QA[:, 0, :], PF[:, base:base + TOK])
                    nc.scalar.activation(SQX, PF[:, base:base + TOK], ACT.Square).then_inc(y_ready, 1)
                    return
                before = [m for m in norm_no if m <= n - 2]
                if before:
                    act.wait_ge(yn_ready, l * NN + (norm_no[before[-1]] + 1))
                parts, w = (D_QK if kind in ("dq", "dk") else P), (KEYS if kind == "dk" else TOK)
                nc.scalar.copy(YB[0:parts, n % 2, 0:w], PF[0:parts, base:base + w])
                nc.scalar.activation(SQ[0:parts, n % 2, 0:w], PF[0:parts, base:base + w], ACT.Square).then_inc(y_ready, 1)

            def std(l, n):
                if n not in norm_no:
                    return
                kind, _ = items[n]
                act.wait_ge(qs_ready, l * NN + (norm_no[n] + 1))
                parts, w = (D_QK if kind in ("dq", "dk") else P), (KEYS if kind == "dk" else TOK)
                size = {"a": A_QK, "b": HD, "c": HD, "d": D_QK}[kind[0]] if kind not in ("qa", "ckv") else \
                    {"qa": 256, "ckv": 128}[kind]
                size = {"qa": 256, "ckv": 128}.get(kind, size)
                nc.scalar.activation(STD[0:parts, n % 2, 0:w], PF[0:parts, 2048:2048 + w], ACT.Sqrt, bias=eps[0:parts],
                                     scale=1.0 / size).then_inc(qstd_ready, 1)

            def exps(l, u):
                br, j, t, hh = units[u]
                if u >= 3:
                    act.wait_ge(t_ready, l * NU + (u - 2))
                for g in maps_of[u]:
                    s = slice(g % 8, g % 8 + 1)
                    act.wait_ge(nm_ready, l * NM + (g + 1))
                    if br == "B":
                        sink = GN[:, G_SINK + 2 * j + hh:G_SINK + 2 * j + hh + 1]
                        nc.scalar.activation(ES[:, s], sink, ACT.Exp, bias=NM_[:, s], scale=1.0)
                    n = P * len(key_tiles(br, t))
                    nc.scalar.activation(PB[:, u % 3, maps[g][1], 0:n], PF[:, 1024 * (g % 2):1024 * (g % 2) + n], ACT.Exp,
                                         bias=NM_[:, s], scale=SCALE[br], accum_out=SU[:, s]).then_inc(exp_done, 1)

            def turned(l, u):
                br, j, t, hh = units[u]
                act.wait_ge(t_ready, l * NU + (u + 1))
                if u >= 2:
                    act.wait_ge(pv_done, l * NU + (u - 1))
                n = P * len(key_tiles(br, t))
                nc.scalar.copy(PT[:, u % 2, 0:n], PF[:, 2048:2048 + n]).then_inc(pt_ready, 1)

            def heads(l, g):
                br, j, t, _ = units[2 * g]
                act.wait_ge(pv_done, l * NU + (2 * g + 2))
                nc.scalar.copy(OUT[:, 2 * "ABCD".index(br) + j, qcols(t)], bank(6 + g % 2, P)).then_inc(o_done, 1)

            with act.Fori(0, DEPTH) as l:
                norm(l, 0)
                act.wait_ge(lam_sum, l + 1)
                nc.scalar.activation(LAME, LAMS, ACT.Exp).then_inc(lam_exp, 1)
                phase_end(act, l, 0)
                for s in range(NI + 1):
                    if s == N_FM:
                        used(l, B_V + N_V - 1)
                        for t in range(TILES):
                            nc.scalar.copy(VT[:, t if t < 4 else 5, :], bank(t if t < 4 else 7)).then_inc(v_out, 1)
                    if s < NI:
                        raw(l, s)
                    if s >= 1:
                        std(l, s - 1)
                used(l, B_KV)
                nc.scalar.copy(VD.rearrange("p a b -> p (a b)"), PF[:, 0:256 * KTILES])
                phase_end(act, l, 1)
                act.dma_start(st_k[l], KT[:, :, NEWK:KEYS]).then_inc(st_out, 16)
                act.dma_start(st_kr[l], KR[0:D_ROPE, NEWK:KEYS]).then_inc(st_out, 16)
                act.dma_start(st_v[l], VT[:, 5, :]).then_inc(st_out, 16)
                for s in range(NU + 4):
                    if s < NU:
                        exps(l, s)
                    if 2 <= s < NU + 2:
                        turned(l, s - 2)
                    if s >= 4 and (s - 4) % 2 == 1:
                        heads(l, (s - 4) // 2)
                phase_end(act, l, 2)
                for j in range(2):
                    nc.scalar.activation(HSQ[:, j, :], OUT[:, j, :], ACT.Square).then_inc(sub_sq, 1)
                for j in range(2):
                    act.wait_ge(sub_ss, l * 2 + (j + 1))
                    nc.scalar.activation(HSTD[:, j, :], PF[:, 1024 * j:1024 * j + TOK], ACT.Sqrt, bias=eps,
                                         scale=1.0 / HD).then_inc(sub_std, 1)
                act.wait_ge(st_out, l * 48 + 48)
                settled(act)
                phase_end(act, l, 3)
                with act.Fori(0, DC) as i:
                    for k in range(4):
                        act.wait_ge(g_ready, l * N_GATE + i * 4 + (k + 1))
                        act.wait_ge(gm_free, l * N_GATE + i * 4 + (k + 1))
                        nc.scalar.activation(SG[:, k % 2, :], PF[:, 1024 * (k % 2):1024 * (k % 2) + TOK],
                                             ACT.Sigmoid).then_inc(sg_ready, 1)
                phase_end(act, l, 4)
                norm(l, 1)
                phase_end(act, l, 5)
                for n in range(N_WQ):
                    act.wait_ge(w_used, l * BLOCKS + (RING + B_WQ + n + 1))
                    nc.scalar.copy(PQ[:, n, :], PF[:, 1024 * (n % 4):1024 * (n % 4) + TOK]).then_inc(q_done, 1)

                def sub_scores_out(t):
                    act.wait_ge(sc_ready, l * TILES + (t + 1))
                    if t >= 1:
                        act.wait_ge(tk_ready, l * TILES + t)
                    nc.scalar.copy(S1, PF[:, 0:2048]).then_inc(s_evac, 1)

                sub_scores_out(0)
                for t in range(TILES):
                    act.wait_ge(cm_ready, l * TILES + (t + 1))
                    nc.scalar.activation(CE, CM, ACT.Exp).then_inc(ce_ready, 1)
                    act.wait_ge(tr_ready, l * TILES + (t + 1))
                    nc.scalar.copy(EWT.rearrange("p a b -> p (a b)"), PF[:, 2048:2048 + 3 * P]).then_inc(ewt_ready, 1)
                    if t + 1 < TILES:
                        sub_scores_out(t + 1)
                    if t >= 1:
                        act.wait_ge(gd_out, l * (16 * TILES) + 16 * t)
                    with act.Fori(0, 16) as i:
                        for b in range(2):
                            act.wait_ge(gmm_done, l * (32 * TILES) + i * 2 + (32 * t + b + 3))
                            nc.scalar.copy(GB[:, :, bass.ds(i * 8 + 4 * b, 4)],
                                           bank(5 + b).rearrange("p (t e) -> p e t", t=4)).then_inc(g_evac, 1)
                act.wait_ge(gd_out, l * (16 * TILES) + 16 * TILES)
                settled(act)
                phase_end(act, l, 6)
                with act.Fori(0, E1 // 8) as i:
                    for k in range(8):
                        act.wait_ge(u_used, l * E1 + i * 8 + (k + 5))
                        if k % 4 == 0:
                            act.wait_ge(o_ready, l * 256 + i * 16 + (2 * k + 8))
                        nc.scalar.activation(HB[:, k, :], PF[:, 1024 * (k % 2):1024 * (k % 2) + TOK],
                                             ACT.Gelu).then_inc(ge_done, 1)
                phase_end(act, l, 7)

        @block.vector
        def _(dve):
            dve.nop().then_inc(mod_copied, 1)
            dve.nop().then_inc(layer_free, 1)
            for _ in range(2):
                dve.nop().then_inc(gm_free, 1)
                dve.nop().then_inc(ac_done, 1)
            dve.wait_ge(c_in, 32)
            dve.wait_ge(cs_sig, 1)
            nc.vector.tensor_tensor(CS[:, :], CS[:, :], SM[:, 144:160], ALU.mult).then_inc(cs_ready, 1)
            dve.wait_ge(x_in, 16)

            def norm(l, which):
                dve.wait_ge(std_ready, l * 2 + (which + 1))
                nc.vector.reciprocal(NRS, NSTD)
                dve.drain()
                for c in range(DC):
                    nc.vector.tensor_tensor(HT[:, c, :], XT[:, c, :], NRS, ALU.mult)
                dve.drain()
                for c in range(DC):
                    for g, span in enumerate((slice(0, LAT), slice(LAT, TOK))):
                        nc.vector.tensor_scalar(HT[:, c, span], HT[:, c, span], SC[:, which, c, g:g + 1],
                                                MD4[:, 3 * which, c, g:g + 1], ALU.mult, ALU.add)

            def target(kind, j):
                return {"aq": lambda: QT[:, j, :], "bq": lambda: QT[:, 2 + j, :], "cq": lambda: QT[:, 4 + j, :],
                        "ak": lambda: KT[:, j, :], "bk": lambda: KT[:, 2, :], "ck": lambda: KT[:, 3, :],
                        "ckv": lambda: KT[:, 4, :], "qa": lambda: QA[:, j, :],
                        "dq": lambda: DQ[0:D_QK, j, :], "dk": lambda: DK[0:D_QK, j, :]}[kind]()

            def head_norm(l, n):
                if n not in norm_no:
                    return
                kind, j = items[n]
                parts, w = (D_QK if kind in ("dq", "dk") else P), (KEYS if kind == "dk" else TOK)
                gcol = {"aq": G_AQ, "ak": G_AK, "bq": G_BQ, "bk": G_BK, "cq": G_CQ, "ck": G_CK, "qa": G_QA + 1,
                        "ckv": G_CKV, "dq": G_DQ, "dk": G_DK}[kind]
                gain = GN[0:parts, gcol:gcol + 1]
                dest = target(kind, j)
                dve.wait_ge(qstd_ready, l * NN + (norm_no[n] + 1))
                nc.vector.reciprocal(RST[0:parts, 0:w], STD[0:parts, n % 2, 0:w])
                dve.drain()
                if kind == "qa":
                    nc.vector.scalar_tensor_tensor(QA[:, 0, :], QA[:, 0, :], GN[:, G_QA:G_QA + 1], RST[:, 0:TOK], ALU.mult, ALU.mult)
                lat = YN[0:parts, rope_no[n] % 2, :] if n in rope_no else dest[:, 0:LAT]
                nc.vector.scalar_tensor_tensor(lat, YB[0:parts, n % 2, 0:LAT], gain, RST[0:parts, 0:LAT], ALU.mult, ALU.mult)
                rest = dest[:, NEWK:KEYS] if kind in ("ak", "bk", "ck", "ckv") else dest[:, LAT:w]
                nc.vector.scalar_tensor_tensor(rest, YB[0:parts, n % 2, LAT:w], gain, RST[0:parts, LAT:w], ALU.mult, ALU.mult)
                dve.drain().then_inc(yn_ready, 1)

            def rope(l, n):
                if n not in rope_no:
                    return
                kind, j = items[n]
                r = rope_no[n]
                parts = D_QK if kind in ("dq", "dk") else P
                tab = {"a": 0, "b": 1, "c": 1, "d": 2}[kind[0]]
                dve.wait_ge(rot_ready, l * NR + (r + 1))
                nc.vector.tensor_tensor(T2[0:parts, :], bank(6, LAT, parts), TG[0:parts, 2 * tab + 1, :], ALU.mult)
                dve.drain()
                dve.wait_ge(t1_ready, l * NR + (r + 1))
                nc.vector.tensor_tensor(target(kind, j)[:, 0:LAT], T1[0:parts, r % 2, :], T2[0:parts, :], ALU.add).then_inc(rope_done, 1)

            def maxima(l, u):
                br, j, t, hh = units[u]
                for g in maps_of[u]:
                    s = slice(g % 8, g % 8 + 1)
                    n = P * len(key_tiles(br, t))
                    at = 1024 * (g % 2)
                    dve.wait_ge(s_ready, l * NM + (g + 1))
                    if br == "B" and t < 4:
                        if t > 0:
                            z = PF[:, at + P:at + 2 * P]
                            nc.vector.tensor_tensor(z, z, band["prev"], ALU.add)
                        if t < 3:
                            z = PF[:, at + n - P:at + n]
                            nc.vector.tensor_tensor(z, z, band["next"], ALU.add)
                        dve.drain()
                    nc.vector.reduce_max(MX[:, s], PF[:, at:at + n], AX.X)
                    dve.drain()
                    if br == "B":
                        sink = GN[:, G_SINK + 2 * j + hh:G_SINK + 2 * j + hh + 1]
                        nc.vector.tensor_scalar(MX[:, s], MX[:, s], SCALE[br], sink, ALU.mult, ALU.max)
                        dve.drain()
                        nc.vector.tensor_scalar(NM_[:, s], MX[:, s], -1.0, None, ALU.mult).then_inc(nm_ready, 1)
                    else:
                        nc.vector.tensor_scalar(NM_[:, s], MX[:, s], -SCALE[br], None, ALU.mult).then_inc(nm_ready, 1)

            def normalise(l, u):
                br, j, t, hh = units[u]
                gs = maps_of[u]
                n = P * len(key_tiles(br, t))
                dve.wait_ge(exp_done, l * NM + (gs[-1] + 1))
                s = slice(gs[0] % 8, gs[0] % 8 + len(gs))
                if br == "B":
                    nc.vector.tensor_tensor(SU[:, s], SU[:, s], ES[:, s], ALU.add)
                    dve.drain()
                nc.vector.reciprocal(RC[:, s], SU[:, s])
                dve.drain()
                p0, p1 = PB[:, u % 3, 0, 0:n], PB[:, u % 3, 1, 0:n]
                if br != "A":
                    nc.vector.tensor_scalar(p0, p0, RC[:, s], None, ALU.mult).then_inc(p_ready, 1)
                    return
                r0, r1 = RC[:, gs[0] % 8:gs[0] % 8 + 1], RC[:, gs[1] % 8:gs[1] % 8 + 1]
                nc.vector.tensor_tensor(r1, r1, NLAM, ALU.mult)
                nc.vector.tensor_scalar(p0, p0, r0, None, ALU.mult)
                dve.drain()
                nc.vector.scalar_tensor_tensor(p0, p1, r1, p0, ALU.mult, ALU.add).then_inc(p_ready, 1)

            def top16(values, indices, scores, spare, n):
                for b in range(n):
                    nc.vector.max(values(b)[:, 0:8], scores(b))
                dve.drain()
                for b in range(n):
                    nc.vector.max_index(indices(b)[:, 0:8], values(b)[:, 0:8], scores(b))
                    nc.vector.match_replace(spare(b), values(b)[:, 0:8], scores(b), LOWEST)
                dve.drain()
                for b in range(n):
                    nc.vector.max(values(b)[:, 8:16], spare(b))
                dve.drain()
                for b in range(n):
                    nc.vector.max_index(indices(b)[:, 8:16], values(b)[:, 8:16], spare(b))
                dve.drain()

            with dve.Fori(0, DEPTH) as l:
                dve.wait_ge(l_in, l * 96 + 16)
                lam = GN[:, G_LAM:G_LAM + 4 * A_QK].rearrange("p (i s k) -> p i s k", i=2, s=2)
                lamp = LAMP.rearrange("p (i k) -> p i k", i=2)
                nc.vector.tensor_tensor(lamp, lam[:, :, 0, :], lam[:, :, 1, :], ALU.mult)
                nc.vector.tensor_tensor(GSUB, GN[:, G_SUB:G_SUB + 1], GN[:, G_LREST:G_LREST + 1], ALU.mult)
                dve.drain()
                nc.vector.reduce_sum(LAMS, lamp, AX.X).then_inc(lam_sum, 1)
                dve.wait_ge(lam_exp, l + 1)
                nc.vector.tensor_tensor(NLAM, LAME[:, 1:2], LAME[:, 0:1], ALU.subtract)
                dve.drain()
                nc.vector.tensor_tensor(NLAM, NLAM, GN[:, G_LINIT:G_LINIT + 1], ALU.subtract)
                with dve.Fori(0, N_ADA // RING) as i:
                    dve.wait_ge(w_used, l * BLOCKS + i * RING + 2 * RING)
                    nc.vector.tensor_copy(MD[:, bass.ds(i * 8, 8)], bank(7, 8)).then_inc(mod_copied, 1)
                dve.drain()
                nc.vector.tensor_tensor(MD[:, :], MD[:, :], GN[:, G_ADAB:G_ADAB + 96], ALU.add)
                dve.drain()
                for which, gcol in enumerate((G_N1, G_N2)):
                    gain = GN[:, gcol:gcol + 16].rearrange("p (c g) -> p c g", c=DC)
                    nc.vector.scalar_tensor_tensor(SC[:, which], MD4[:, 3 * which + 1], 1.0, gain, ALU.add, ALU.mult)
                dve.drain()
                norm(l, 0)
                phase_end(dve, l, 0)
                dve.wait_ge(l_in, l * 96 + 80)
                for s in range(1, NI + 2):
                    if s <= NI:
                        head_norm(l, s - 1)
                    if s >= 2:
                        rope(l, s - 2)
                phase_end(dve, l, 1)
                for s in range(NU + 1):
                    if s < NU:
                        maxima(l, s)
                    if s >= 1:
                        normalise(l, s - 1)
                phase_end(dve, l, 2)
                for j in range(2):
                    dve.wait_ge(sub_std, l * 2 + (j + 1))
                    nc.vector.reciprocal(HRS[:, j, :], HSTD[:, j, :])
                    dve.drain()
                    nc.vector.scalar_tensor_tensor(OUT[:, j, :], OUT[:, j, :], GSUB, HRS[:, j, :], ALU.mult, ALU.mult)
                phase_end(dve, l, 3)
                with dve.Fori(0, DC) as i:
                    for k in range(4):
                        dve.wait_ge(sg_ready, l * N_GATE + i * 4 + (k + 1))
                        dve.wait_ge(w_used, l * BLOCKS + i * 4 + (RING + B_GATE + k + 1))
                        br = PF[:, 2048 + 1024 * (k % 2):2048 + 1024 * (k % 2) + TOK]
                        if k == 0:
                            nc.vector.tensor_tensor(YS[:, i, :], SG[:, 0, :], br, ALU.mult).then_inc(gm_free, 1)
                        else:
                            nc.vector.tensor_tensor(GM[:, k % 2, :], SG[:, k % 2, :], br, ALU.mult)
                            dve.drain()
                            nc.vector.tensor_tensor(YS[:, i, :], YS[:, i, :], GM[:, k % 2, :], ALU.add).then_inc(gm_free, 1)
                for n in range(N_WOUT):
                    dve.wait_ge(w_used, l * BLOCKS + (RING + B_WOUT + n + 1))
                    for g, (lo, hi) in enumerate(((0, LAT), (LAT, TOK))):
                        last = nc.vector.scalar_tensor_tensor(XT[:, n, lo:hi], PF[:, 1024 * (n % 2) + lo:1024 * (n % 2) + hi],
                                                              MD4[:, 2, n, g:g + 1], XT[:, n, lo:hi], ALU.mult, ALU.add)
                    last.then_inc(wo_done, 1)
                phase_end(dve, l, 4)
                norm(l, 1)
                phase_end(dve, l, 5)
                I1U, CIU, CAU, CBU = (x.bitcast(U32) for x in (I1, CI, CA, CB))
                s1, s2 = (x.rearrange("p (b k) -> p b k", b=SUB) for x in (S1, S2))
                c1, c2 = (x.rearrange("p (h k) -> p h k", h=PH) for x in (S1, S2))
                m1, m2 = (x.rearrange("p (h s k) -> p h s k", h=PH, s=TOPK) for x in (S1, S2))
                V4 = V1.rearrange("p (h s) k -> p h s k", s=2)
                F4 = I1F.rearrange("p (h s) k -> p h s k", s=2)
                all4 = [P, PH, TOPK, TOPK]
                for t in range(TILES):
                    dve.wait_ge(s_evac, l * TILES + (t + 1))
                    settled(dve)
                    top16(lambda b: V1[:, b, :], lambda b: I1U[:, b, :], lambda b: s1[:, b, :], lambda b: s2[:, b, :], SUB)
                    nc.vector.tensor_copy(I1F, I1U)
                    nc.vector.tensor_tensor(m1, V4[:, :, 0, :].unsqueeze(3).broadcast_to(all4),
                                            V4[:, :, 1, :].unsqueeze(2).broadcast_to(all4), ALU.add)
                    dve.drain()
                    top16(lambda h: CV[:, h, :], lambda h: CIU[:, h, :], lambda h: c1[:, h, :], lambda h: c2[:, h, :], PH)
                    nc.vector.tensor_tensor(CM, CV, CV[:, :, 0:1].broadcast_to([P, PH, TOPK]), ALU.subtract).then_inc(cm_ready, 1)
                    nc.vector.tensor_single_scalar(CAU, CIU, 4, ALU.logical_shift_right)
                    nc.vector.tensor_single_scalar(CBU, CIU, 15, ALU.bitwise_and)
                    dve.drain()
                    nc.vector.tensor_copy(CAF, CAU)
                    nc.vector.tensor_copy(CBF, CBU)
                    dve.drain()
                    for side, place in enumerate((CAF, CBF)):
                        nc.vector.tensor_tensor(m1, place.unsqueeze(3).broadcast_to(all4),
                                                iota16.unsqueeze(1).unsqueeze(1).broadcast_to(all4), ALU.is_equal)
                        dve.drain()
                        nc.vector.tensor_tensor(m2, m1, F4[:, :, side, :].unsqueeze(2).broadcast_to(all4), ALU.mult)
                        dve.drain()
                        nc.vector.reduce_sum(EW[:, side, :].rearrange("p (h k) -> p h k", h=PH), m2, AX.X)
                        dve.drain()
                    dve.wait_ge(ce_ready, l * TILES + (t + 1))
                    nc.vector.reduce_sum(CSUM, CE, AX.X)
                    dve.drain()
                    nc.vector.reciprocal(CRC, CSUM)
                    dve.drain()
                    nc.vector.tensor_tensor(EW[:, 2, :].rearrange("p (h k) -> p h k", h=PH), CE,
                                            CRC.unsqueeze(2).broadcast_to([P, PH, TOPK]), ALU.mult)
                    dve.drain().then_inc(tk_ready, 1)
                    dve.wait_ge(ewt_ready, l * TILES + (t + 1))
                    settled(dve)
                    with dve.Fori(0, 16) as i:
                        for b in range(2):
                            dve.wait_ge(gmm_done, l * (32 * TILES) + i * 2 + (32 * t + b + 1))
                            for k in range(4):
                                tok = bass.ds(i * 8 + (4 * b + k), 1)
                                nc.vector.tensor_scalar(HOT[:, b, 2 * k, :], iota, EWT[:, 1, tok], None, ALU.is_equal)
                                last = nc.vector.tensor_scalar(HOT[:, b, 2 * k + 1, :], iota, EWT[:, 0, tok], EWT[:, 2, tok],
                                                               ALU.is_equal, ALU.mult)
                            last.then_inc(hot_ready, 1)
                phase_end(dve, l, 6)
                nc.vector.memset(AC.rearrange("p a b -> p (a b)"), 0.0)
                with dve.Fori(0, E1 // 8) as i:
                    for k in range(8):
                        dve.wait_ge(ge_done, l * E1 + i * 8 + (k + 3))
                        if k % 4 == 0:
                            dve.wait_ge(g_in[k // 4], l * (16 * E1 // 8) + i * 16 + 16)
                        nc.vector.tensor_tensor(HB[:, k, :], HB[:, k, :], GT[:, k, :], ALU.mult).then_inc(h_ready, 1)
                    for half in range(2):
                        dve.drain()
                        for d in range(DC):
                            dve.wait_ge(o_ready, l * 256 + i * 16 + (16 + 8 * half + d + 1))
                            nc.vector.tensor_tensor(AC[:, d, :], AC[:, d, :], PF[:, 2048 + 1024 * (d % 2):2048 + 1024 * (d % 2) + TOK],
                                                    ALU.add).then_inc(ac_done, 1)
                dve.drain()
                for c in range(DC):
                    for g, (lo, hi) in enumerate(((0, LAT), (LAT, TOK))):
                        nc.vector.scalar_tensor_tensor(XT[:, c, lo:hi], AC[:, c, lo:hi], MD4[:, 5, c, g:g + 1],
                                                       XT[:, c, lo:hi], ALU.mult, ALU.add)
                phase_end(dve, l, 7)
                dve.drain().then_inc(layer_free, 1)

        @block.gpsimd
        def _(pool):
            pool.wait_ge(c_in, 32)
            with pool.Fori(0, DEPTH) as l:
                phase_end(pool, l, 0)
                pool.wait_ge(l_in, l * 96 + 80)
                for n, r in rope_no.items():
                    kind, _ = items[n]
                    parts = D_QK if kind in ("dq", "dk") else P
                    tab = {"a": 0, "b": 1, "c": 1, "d": 2}[kind[0]]
                    pool.wait_ge(yn_ready, l * NN + (norm_no[n] + 1))
                    if r >= 2:
                        pool.wait_ge(rope_done, l * NR + (r - 1))
                    nc.gpsimd.tensor_tensor(T1[0:parts, r % 2, :], YN[0:parts, r % 2, :], TG[0:parts, 2 * tab, :],
                                            ALU.mult).then_inc(t1_ready, 1)
                for n in range(1, NBAR):
                    phase_end(pool, l, n)


def key_spans(br, t):
    if t == TILES - 1:
        return [(NEWK, KEYS)]
    if br == "B":
        return [(LAT, NEWK), (P * max(0, t - 1), P * min(4, t + 2))]
    return [(0, LAT), (LAT, NEWK)]


def key_tiles(br, t):
    return [k for lo, hi in key_spans(br, t) for k in range(lo // P, hi // P)]


def make_consts():
    c = np.zeros((P, C_ALL), np.float32)
    i = np.arange(P)
    c[:, C_ONES:C_ONES + P] = 1
    c[:, C_G32:C_G32 + P] = i[:, None] // 32 == i[None] // 32
    c[:, C_G64:C_G64 + P] = i[:, None] // 64 == i[None] // 64

    def rotation(at, size, start, end):
        q = size // 4
        for head in range(start, end, size):
            for half in range(2):
                for r in range(q):
                    x0, x1 = head + half * 2 * q + r, head + half * 2 * q + q + r
                    c[x1, at + x0] = -1
                    c[x0, at + x1] = 1

    rotation(C_RA, A_QK, 0, P)
    rotation(C_RB, HD, 0, P)
    rotation(C_RD, D_ROPE, D_NOPE, D_QK)
    c[:, C_ID:C_ID + P] = np.eye(P)
    c[:, C_PREV:C_PREV + P] = np.where(i[None] >= i[:, None], 0, NEG)
    c[:, C_NEXT:C_NEXT + P] = np.where(i[None] <= i[:, None], 0, NEG)
    c[:, C_IOTA:C_IOTA + P] = i[None]
    for r in range(D_ROPE):
        c[r, C_SEL + D_NOPE + r] = 1
    c[:, C_I16:C_I16 + 16] = np.arange(16)
    c[:, C_EPS] = EPS
    return c


def make_trig():
    out = np.zeros((P, 6, LAT), np.float32)
    tok = np.arange(LAT)
    row, col = (tok // 64).astype(np.float32), (tok % 64).astype(np.float32)
    for n, (size, start, rows) in enumerate(((A_QK, 0, P), (HD, 0, P), (D_ROPE, D_NOPE, D_QK))):
        q = size // 4
        inv = (np.float32(10000.0) ** (-np.arange(q, dtype=np.float32) / np.float32(q))).astype(np.float32)
        out[:, 2 * n] = 1
        for p in range(start, rows):
            f = (p - start) % size
            ang = (row if f < 2 * q else col) * inv[f % q]
            out[p, 2 * n] = np.cos(ang.astype(np.float64))
            out[p, 2 * n + 1] = np.sin(ang.astype(np.float64))
    return out


def blocks_of(w):
    k, n = w.shape
    return np.ascontiguousarray(w.reshape(k // P, P, n // P, P).transpose(2, 1, 0, 3)).reshape(n // P, P, k)


def kernel(**inputs):
    import concourse.bacc as bacc
    from concourse.bass_utils import run_bass_kernel_spmd

    x = {k: np.asarray(v) for k, v in inputs.items()}
    L = DEPTH

    def chunked(v):
        return v.reshape(DC, P).T

    xall = np.concatenate([x["x_sample"][0], x["x_prompt"][0]])
    xT = xall.T.reshape(DC, P, TOK).transpose(1, 0, 2)
    csT = np.stack([chunked(x["c"][0]), chunked(x["c_ctx"])], axis=2).reshape(P, 16)

    sizes = [256, 256, 256, 256, 128, 128, 256, 128, 128, 256, 128, 32, 4096]
    offs = np.concatenate([[0], np.cumsum(sizes)])
    swap = np.concatenate([np.arange(64) + 64 * h for h in (0, 2, 1, 3)])
    ada, wfm, wv, wdq, wkv, wgate, wout, wq, vecs, subk = ([] for _ in range(10))
    for l in range(L):
        ada.append(blocks_of(x["ada_w"][l]))
        aq, ak, av, bq, bk, bv, cq, ck, cv, qa, ckv, kr, gt = (x["w_in"][l][:, offs[i]:offs[i + 1]] for i in range(13))
        kr = np.concatenate([kr, np.zeros((D, P - D_ROPE), np.float32)], axis=1)
        wfm.append(blocks_of(np.concatenate([aq, ak, bq[:, swap], bk, cq[:, swap], ck, qa, ckv, kr], axis=1)))
        v = np.concatenate([av, bv, cv], axis=1)
        wv.append(v.reshape(N_V, 2, P, 512).transpose(0, 2, 1, 3).reshape(N_V, P, 1024))
        wdq.append(x["w_d_qb"][l].reshape(2, P, HEADS * D_QK).transpose(1, 0, 2).reshape(P, -1))
        kv = x["w_d_kvb"][l].reshape(P, HEADS, 128)
        wk = np.concatenate([kv[:, :, :64], np.zeros((P, HEADS, D_ROPE), np.float32)], axis=2).reshape(P, -1)
        wkv.append(np.concatenate([wk, kv[:, :, 64:].reshape(P, -1)], axis=1))
        g = blocks_of(gt).reshape(4, DC, P, D)
        b = x["w_branch"][l].reshape(4, 2, P, DC, P).transpose(3, 0, 2, 1, 4).reshape(DC, 4, P, 2 * P)
        wgate.append(np.concatenate([g.transpose(1, 0, 2, 3), b], axis=3).reshape(N_GATE, P, SLOT))
        wout.append(blocks_of(x["w_out"][l]))
        wq.append(blocks_of(x["peer_wq"][l]))
        subk.append(x["peer_subkeys"][l].transpose(3, 0, 1, 2).reshape(P, SUB, PK))
        lam_init = 0.8 - 0.6 * math.exp(-0.3 * l)
        vec = np.zeros((P, G_ALL), np.float32)
        twice = lambda m: np.repeat(m, 2, axis=1)
        vec[:, G_ADAB:G_ADAB + 96] = twice(x["ada_b"][l].reshape(48, P).T)
        vec[:, G_N1:G_N1 + 16] = twice(chunked(x["norm1_g"][l]))
        vec[:, G_N2:G_N2 + 16] = twice(chunked(x["norm2_g"][l]))
        for c, (name, i, n) in {G_AQ: ("a_qk_g", 0, 4), G_AK: ("a_qk_g", 1, 4), G_BQ: ("b_qk_g", 0, 2), G_BK: ("b_qk_g", 1, 2),
                                G_CQ: ("c_qk_g", 0, 2), G_CK: ("c_qk_g", 1, 2)}.items():
            vec[:, c] = np.tile(x[name][l, i], n)
        vec[:, G_QA:G_QA + 2] = x["d_qnorm_g"][l].reshape(2, P).T
        vec[:, G_CKV] = x["d_kvnorm_g"][l]
        vec[:D_QK, G_DQ] = x["d_qk_g"][l, 0]
        vec[:D_QK, G_DK] = x["d_qk_g"][l, 1]
        vec[:, G_SUB] = np.tile(x["a_subln_g"][l], 2)
        vec[:, G_LAM:G_LAM + 128] = x["a_lam"][l].reshape(1, 128)
        vec[:, G_SINK:G_SINK + 4] = x["b_sink"][l][None]
        vec[:, G_LINIT] = lam_init
        vec[:, G_LREST] = 1.0 - lam_init
        vecs.append(vec)

    def keys_of(name, blocks):
        k = x[name][0].reshape(L, PAST, blocks, P)
        return k.transpose(0, 3, 2, 1)

    cache_k = np.concatenate([keys_of("cache_a_k", 2), keys_of("cache_b_k", 1), keys_of("cache_c_k", 1),
                              keys_of("cache_d_ckv", 1)], axis=2)
    cache_kr = x["cache_d_krope"][0].transpose(0, 2, 1)
    cache_v = np.concatenate([x[f"cache_{b}_v"][0].reshape(L, PAST, -1) for b in "abc"], axis=2)
    uT = x["peer_u"].reshape(L, E1, P, DC, P).transpose(0, 1, 4, 3, 2).reshape(L, E1, P, D)
    vtab = x["peer_v"].reshape(L, E1, P, D)

    ins = dict(xT=xT, csT=csT, consts=make_consts(), trig=make_trig(), vecs=np.stack(vecs), ada=np.stack(ada),
               wfm=np.stack(wfm), wv=np.stack(wv), wdq=np.stack(wdq), wkv=np.stack(wkv), wgate=np.stack(wgate),
               wout=np.stack(wout), wq=np.stack(wq), subk=np.stack(subk), uT=uT, vtab=vtab, cache_k=cache_k,
               cache_kr=cache_kr, cache_v=cache_v)
    outs = dict(yT=(P, DC, TOK), st_k=(L, P, 5, CTX), st_kr=(L, D_ROPE, CTX), st_v=(L, CTX, 512))
    nc = bacc.Bacc("TRN2", target_bir_lowering=False, num_devices=1,
                   dynamic_dma_scratch_size=1024)
    arrays, args = {}, {}
    for name, a in ins.items():
        arrays[f"in_{name}"] = a = np.ascontiguousarray(a)
        args[name] = nc.dram_tensor(f"in_{name}", a.shape, mybir.dt.from_np(a.dtype), kind="ExternalInput").ap()
    for name, shape in outs.items():
        args[name] = nc.dram_tensor(f"out_{name}", shape, F32, kind="ExternalOutput").ap()
    build(nc, **args)
    r = run_bass_kernel_spmd(nc, [arrays], core_ids=[0]).results[0]

    y = r["out_yT"].transpose(1, 0, 2).reshape(D, TOK).T
    sk, skr, sv = r["out_st_k"], r["out_st_kr"], r["out_st_v"]

    def keys(blocks, *shape):
        return sk[:, :, blocks].transpose(0, 3, 2, 1).reshape((1, L, CTX) + shape)

    return (y[LAT:].reshape(1, CTX, D), y[:LAT].reshape(1, LAT, D),
            keys([0, 1], 4, 2, A_QK), sv[:, :, 0:256].reshape(1, L, CTX, 4, 64),
            keys([2], 2, 64), sv[:, :, 256:384].reshape(1, L, CTX, 2, 64),
            keys([3], 2, 64), sv[:, :, 384:512].reshape(1, L, CTX, 2, 64),
            keys([4], 128), skr.transpose(0, 2, 1).reshape(1, L, CTX, D_ROPE))
```

```python
import math
from contextlib import ExitStack

import numpy as np

import concourse.bass as bass
from concourse import mybir

F32 = mybir.dt.float32
F32R = mybir.dt.float32r
U32 = mybir.dt.uint32
ALU = mybir.AluOpType
ACT = mybir.ActivationFunctionType
AX = mybir.AxisListType

P = 128
D = 1024
DC = D // P
DEPTH = 2
LAT, CTX, PAST = 512, 128, 128
TOK = LAT + CTX
KEYS = LAT + PAST + CTX
NEWK = LAT + PAST
TILES = TOK // P
KTILES = KEYS // P
EPS = 1e-6
NEG = -1e30
LOWEST = -3.0e38

A_QK, HD, D_QK, D_NOPE, D_ROPE = 32, 64, 96, 64, 32
HEADS = 4
SCALE = {"A": A_QK ** -0.5, "B": HD ** -0.5, "C": HD ** -0.5, "D": D_QK ** -0.5}

PH, PK, TOPK = 8, 128, 16
SUB = 2 * PH
E1 = PK
AHEAD, BESIDE = 8, 4
PER_TILE = AHEAD + BESIDE

RING = 4
SLOT = 1280
N_ADA1, N_ADA2, N_FM, N_V, N_GATE, N_WOUT, N_WQ = 16, 32, 14, 4, 32, 8, 16
N_ADA = N_ADA1 + N_ADA2
B_FM = N_ADA1
B_V = B_FM + N_FM
B_DQ = B_V + N_V
B_KV = B_DQ + 1
B_ADA2 = B_KV + 1
B_GATE = B_ADA2 + N_ADA2
B_WOUT = B_GATE + N_GATE
B_WQ = B_WOUT + N_WOUT
BLOCKS = B_WQ + N_WQ
assert BLOCKS % RING == 0 and B_GATE % RING == 0 and B_ADA2 % RING == 0


def loads(n):
    pairs = sum(m % RING == n % RING for m in [*range(N_ADA1), *range(B_ADA2, B_GATE)] if m < n)
    return n // RING - (pairs if n % 2 else 0)


PER_SLOT = [loads(BLOCKS + k) for k in range(RING)]
SPLIT_NO = {n: i for i, n in enumerate([*range(B_FM, B_DQ), *range(B_GATE, B_WOUT), *range(B_WQ, BLOCKS)])}
N_SPLIT = len(SPLIT_NO)

G_ADAB, G_N1, G_N2 = 0, 96, 112
G_AQ, G_AK, G_BQ, G_BK, G_CQ, G_CK = range(128, 134)
G_QA, G_CKV, G_DQ, G_DK, G_SUB = 134, 136, 137, 138, 139
G_LAM, G_SINK, G_LINIT, G_LREST = 140, 268, 272, 273
G_ALL = 274

C_ONES, C_G32, C_G64, C_RA, C_RB, C_RD, C_ID, C_PREV, C_NEXT, C_IOTA, C_SEL = [P * i for i in range(11)]
C_I16 = P * 11
C_EPS = C_I16 + 16
C_ALL = C_EPS + 1
TRIG = 6 * LAT


class Arena:

    def __init__(self, tensor, start, size):
        self.tensor, self.at, self.end = tensor, start, size

    def take(self, *dims):
        n = int(np.prod(dims))
        ap = self.tensor[:, self.at:self.at + n]
        self.at += n
        assert self.at <= self.end, (self.at, self.end)
        if len(dims) == 2:
            ap = ap.rearrange("p (a b) -> p a b", a=dims[0])
        if len(dims) == 3:
            ap = ap.rearrange("p (a b c) -> p a b c", a=dims[0], b=dims[1])
        return ap


AFTER = 4
EARLY = TILES * PER_TILE + AFTER
LATE = E1 - EARLY
HALF = TOK // TILES // 2
BATCHES = HALF // 4
assert EARLY % 4 == 0 and LATE % 4 == 0 and BATCHES == 2 * DC and BESIDE == 4 and AHEAD % 2 == 0


def build(nc, xT, csT, consts, trig, vecs, ada, wfm, wv, wdq, wkv, wgate, wout, wq, subk, uT, vtab,
          cache_k, cache_kr, cache_v, yT, st_k, st_kr, st_v):
    gates = nc.dram_tensor("gates_by_expert", (E1, P, TOK), F32, kind="Internal").ap()
    early_rows = nc.dram_tensor("early_activations", (EARLY, P, TOK), F32, kind="Internal").ap()
    sub_rows = nc.dram_tensor("sub_key_scores", (TILES, P, SUB * PK), F32, kind="Internal").ap()

    items = ([("aq", 0), ("aq", 1), ("ak", 0), ("ak", 1), ("bq", 0), ("bq", 1), ("bk", 0), ("cq", 0), ("cq", 1),
              ("ck", 0), ("qa", 0), ("qa", 1), ("ckv", 0), ("kr", 0)]
             + [("dq", h) for h in range(HEADS)] + [("dk", h) for h in range(HEADS)])
    NI = len(items)
    ROPED = {"aq", "ak", "bq", "bk", "cq", "ck", "dq", "dk"}
    norm_no = {n: i for i, n in enumerate(n for n in range(NI) if items[n] not in (("qa", 0), ("kr", 0)))}
    rope_no = {n: i for i, n in enumerate(n for n in range(NI) if items[n][0] in ROPED)}
    NN, NR = len(norm_no), len(rope_no)
    at_item = {it: n for n, it in enumerate(items)}

    units = [(br, j, t, hh) for br in "ABCD" for j in range(2) for t in range(TILES) for hh in range(2)]
    maps = [(u, m) for u, x in enumerate(units) for m in range(2 if x[0] == "A" else 1)]
    maps_of = [[g for g, (uu, _) in enumerate(maps) if uu == u] for u in range(len(units))]
    NU, NM = len(units), len(maps)
    NBAR = 9

    with ExitStack() as ctx:
        def sb(name, shape, dt=F32):
            return ctx.enter_context(nc.sbuf_tensor(name, shape, dt))

        def sem(name):
            return ctx.enter_context(nc.semaphore(name))

        XT = sb("XT", [P, DC, TOK])
        HT = sb("HT", [P, DC, TOK])
        HR = sb("HR", [P, 2, DC, TOK], F32R)
        UR = sb("UR", [P, 2, 2, D], F32R)
        WR = sb("WR", [P, RING, SLOT])
        CN = sb("CN", [P, C_ALL])
        GN = sb("GN", [P, G_ALL])
        MD = sb("MD", [P, 96])
        CS = sb("CS", [P, 16])
        SM = sb("SM", [P, 160])
        IDLE = sb("IDLE", [P, 64])
        AF = 25300
        with nc.sbuf_tensor("AR", [P, AF], F32) as AR:
            pass
        VR = sb("VR", [P, 4, 2, D], F32R)
        HB = sb("HB", [P, 4, 2, TOK], F32R)
        GT = sb("GT", [P, 4, TOK])
        HW = sb("HW", [P, 4, TOK])
        PS = ctx.enter_context(nc.psum_tensor("PS", [P, 8, 512], F32))
        PF = PS[:, :, :].rearrange("p a b -> p (a b)")

        def bank(b, n=512, parts=P):
            return PF[0:parts, 512 * b:512 * b + n]

        ones, grp32, grp64 = (CN[:, c:c + P] for c in (C_ONES, C_G32, C_G64))
        rot32, rot64 = CN[:, C_RA:C_RA + P], CN[:, C_RB:C_RB + P]
        rot96 = CN[0:D_QK, C_RD:C_RD + D_QK]
        ident = CN[:, C_ID:C_ID + P]
        band = {"prev": CN[:, C_PREV:C_PREV + P], "next": CN[:, C_NEXT:C_NEXT + P]}
        iota = CN[:, C_IOTA:C_IOTA + P]
        sel_kr = CN[0:D_ROPE, C_SEL:C_SEL + D_QK]
        iota16 = CN[:, C_I16:C_I16 + 16]
        eps = CN[:, C_EPS:C_EPS + 1]
        MOD2 = PF[:, 2560 + 256:2560 + 256 + 2 * N_ADA2]
        MD4 = MD[:, :].rearrange("p (w c g) -> p w c g", w=6, c=DC)
        SC = SM[:, 0:32].rearrange("p (n c g) -> p n c g", n=2, c=DC)
        LAMP, LAMS, LAME, NLAM, GSUB = SM[:, 32:96], SM[:, 96:98], SM[:, 98:100], SM[:, 100:101], SM[:, 101:102]
        MX, NM_, SU, RC, ES = (SM[:, 104 + 8 * i:112 + 8 * i] for i in range(5))

        a = Arena(AR, 0, AF)
        KT = a.take(5, KEYS)
        KR = a.take(KEYS)
        DK = a.take(HEADS, KEYS)
        QT = a.take(6, TOK)
        DQ = a.take(HEADS, TOK)
        QA = a.take(2, TOK)
        VT = a.take(KTILES, 512)
        VD = a.take(KTILES, 256)
        shared = a.at
        q_ = Arena(AR, shared, AF)
        HF = HT[:, :, :].rearrange("p a b -> p (a b)")
        TG = HF[:, 0:6 * LAT].rearrange("p (a b) -> p a b", a=6)
        SQX = HF[:, 6 * LAT:6 * LAT + TOK]
        YB, SQ, YN = q_.take(2, KEYS), q_.take(2, KEYS), q_.take(2, LAT)
        RST = q_.take(KEYS)
        STD = VD.rearrange("p a b -> p (a b)").rearrange("p (a b) -> p a b", a=2)
        T1 = HF[:, 6 * LAT + TOK:8 * LAT + TOK].rearrange("p (a b) -> p a b", a=2)
        T2 = RST[:, 0:LAT]
        OUT = HT
        t_ = Arena(AR, shared, AF)
        PB = t_.take(3, 2, 640)
        PT = t_.take(2, 640)
        u_ = Arena(AR, shared, AF)
        HSQ, HSTD, HRS = u_.take(2, TOK), u_.take(2, TOK), u_.take(2, TOK)
        g_ = Arena(AR, 0, shared)
        YS, SG, GM = g_.take(DC, TOK), g_.take(2, TOK), g_.take(2, TOK)
        n_ = Arena(AR, 0, AF)
        NSQ, NSTD, NRS = n_.take(DC, TOK), n_.take(TOK), n_.take(TOK)
        p_ = Arena(AR, 0, AF)
        PQ, SK, SS = p_.take(SUB, TOK), p_.take(SUB, PK), p_.take(2, SUB * PK)
        p_ = Arena(AR, 0, AF)
        V1, I1, I1F = p_.take(SUB, TOPK), p_.take(SUB, TOPK), p_.take(SUB, TOPK)
        CV, CI, CM, CE = p_.take(PH, TOPK), p_.take(PH, TOPK), p_.take(PH, TOPK), p_.take(PH, TOPK)
        CA, CB, CAF, CBF = p_.take(PH, TOPK), p_.take(PH, TOPK), p_.take(PH, TOPK), p_.take(PH, TOPK)
        EW = p_.take(3, P)
        EWT = p_.take(3, P)
        CSUM, CRC = p_.take(PH), p_.take(PH)
        HOT = p_.take(2, 8, P)
        GB = p_.take(P, P)
        AS = p_.take(2, TOK)
        S1, S2 = (HF[:, 2048 * i:2048 * (i + 1)] for i in range(2))
        AC = HT

        bar, layer_free = sem("phase_ends"), sem("layer_free")
        c_in, l_in, x_in = sem("consts_in"), sem("layer_in"), sem("x_in")
        w_in = [sem(f"weights_in{k}") for k in range(RING)]
        w_used = sem("weights_used")
        cs_ready, mod_copied, lam_sum, lam_exp = sem("cs_ready"), sem("mod_copied"), sem("lam_sum"), sem("lam_exp")
        cs_sig = sem("cs_sig")
        sq_ready, ss_ready, std_ready = sem("norm_squares"), sem("norm_sums"), sem("norm_std")
        pj_ready, y_ready, qs_ready, qstd_ready = sem("proj_ready"), sem("raw_ready"), sem("head_sums"), sem("head_std")
        yn_ready, rot_ready, t1_ready, rope_done = sem("normed"), sem("rotated"), sem("cos_part"), sem("rope_done")
        v_out = sem("v_out")
        st_out = sem("states_out")
        s_ready, nm_ready, exp_done, p_ready = sem("scores"), sem("neg_max"), sem("exp_done"), sem("probs")
        t_ready, pt_ready, pv_done, o_done = sem("probs_turned"), sem("probs_t_out"), sem("pv_done"), sem("heads_out")
        sub_sq, sub_ss, sub_std = sem("sub_squares"), sem("sub_sums"), sem("sub_std")
        g_ready, sg_ready, gm_free = sem("gate_ready"), sem("sigmoid_ready"), sem("gated")
        wo_done, q_done = sem("residual_added"), sem("peer_q_out")
        sc_ready, s_evac, cm_ready, ce_ready, tk_ready = (sem(n) for n in (
            "sub_scores", "sub_scores_out", "chosen_minus_max", "chosen_exp", "choice_ready"))
        tr_ready, ewt_ready, hot_ready, gmm_done, g_evac, gd_out = (sem(n) for n in (
            "choice_turned", "choice_t_out", "one_hots", "gates_spread", "gates_copied", "gates_stored"))
        ht_ready, hs_ready, hh_ready, hr_ready = sem("h_scaled"), sem("h_shifted"), sem("h_high"), sem("h_parts")
        hi_ready, split = sem("high_parts"), sem("blocks_split")
        ss_out, ss_in = [sem(f"sub_scores_stored{k}") for k in range(2)], sem("sub_scores_in")
        uh_ready, vh_ready, u_split, v_split = (sem(n) for n in ("u_high", "v_high", "u_split", "v_split"))
        u_in = [sem(f"u_in{k}") for k in range(2)]
        v_in, g_in = [sem(f"v_in{k}") for k in range(2)], [sem(f"g_in{k}") for k in range(2)]
        u_used, ge_done, h_ready, o_ready, ac_done = (sem(n) for n in (
            "u_used", "gelu_done", "gated_gelu", "expert_sums", "expert_sums_added"))
        a_out, a_in = ([sem(f"{n}{k}") for k in range(2)] for n in ("activations_stored", "activations_in"))
        y_out = sem("y_out")

        idle_cells = iter(range(64))

        def settled(eng):
            n = next(idle_cells)
            cell = IDLE[:, n:n + 1]
            if eng.engine == nc.vector.engine:
                nc.vector.memset(cell, 0.0)
            elif eng.engine == nc.scalar.engine:
                nc.scalar.copy(cell, eps)
            elif eng.engine == nc.gpsimd.engine:
                nc.gpsimd.tensor_tensor(cell, eps, eps, ALU.mult)
            else:
                nc.tensor.matmul(bank(7)[:, 508:510], ident, iota[:, 0:2], start=True, stop=True)

        def phase_end(eng, l, n):
            eng.drain().then_inc(bar, 1)
            eng.wait_ge(bar, l * (4 * NBAR) + 4 * (n + 1))
            settled(eng)

        def tiles_of(k):
            return (TILES + 1 - k) // 2

        def qcols(t):
            return slice(P * t, P * t + P)

        block = ctx.enter_context(nc.Block())

        @block.sync
        def _(sp):
            sp.dma_start(CN[:, :], consts).then_inc(c_in, 16)
            sp.dma_start(CS[:, :], csT).then_inc(c_in, 16)
            sp.dma_start(XT[:, :, :], xT).then_inc(x_in, 16)

            def load(l, n, dst, src):
                sp.wait_ge(w_used, l * BLOCKS + (n + 1))
                sp.dma_start(dst, src).then_inc(w_in[n % RING], 16)

            with sp.Fori(0, DEPTH) as l:
                sp.wait_ge(layer_free, l + 1)
                sp.dma_start(GN[:, :], vecs[l]).then_inc(l_in, 16)

                def load_ada(i, k, first, at):
                    sp.wait_ge(w_used, l * BLOCKS + i * RING + (at + k + 2))
                    sp.dma_start(WR[:, k:k + 2, 0:D], ada[l, bass.ds(i * RING + (first + k), 2)].rearrange("a b t -> b a t")
                                 ).then_inc(w_in[k], 16)

                with sp.Fori(0, N_ADA1 // RING) as i:
                    for k in (0, 2):
                        load_ada(i, k, 0, 0)
                for n in range(RING):
                    load(l, B_FM + n, WR[:, (B_FM + n) % RING, 0:D], wfm[l, n])
                sp.wait_ge(hr_ready, l * (2 * DC) + DC)
                sp.dma_start(TG[:, :, :], trig).then_inc(l_in, 16)
                sp.dma_start(KT[:, :, LAT:NEWK], cache_k[l]).then_inc(l_in, 16)
                sp.dma_start(KR[0:D_ROPE, LAT:NEWK], cache_kr[l]).then_inc(l_in, 16)
                sp.dma_start(VT[:, 4, :], cache_v[l]).then_inc(l_in, 16)
                for n in range(RING, N_FM):
                    load(l, B_FM + n, WR[:, (B_FM + n) % RING, 0:D], wfm[l, n])
                for n in range(N_V):
                    load(l, B_V + n, WR[:, (B_V + n) % RING, 0:D], wv[l, n])
                load(l, B_DQ, WR[:, B_DQ % RING, 0:2 * HEADS * D_QK], wdq[l])
                load(l, B_KV, WR[:, B_KV % RING, 0:HEADS * (D_QK + HD)], wkv[l])
                with sp.Fori(0, N_ADA2 // RING) as i:
                    for k in (0, 2):
                        load_ada(i, k, N_ADA1, B_ADA2)
                with sp.Fori(0, N_GATE // RING) as i:
                    for k in range(RING):
                        sp.wait_ge(w_used, l * BLOCKS + i * RING + (B_GATE + k + 1))
                        sp.dma_start(WR[:, k, 0:SLOT], wgate[l, i * RING + k]).then_inc(w_in[k], 16)
                for n in range(N_WOUT):
                    load(l, B_WOUT + n, WR[:, (B_WOUT + n) % RING, 0:D], wout[l, n])
                for n in range(N_WQ):
                    if n == RING:
                        sp.wait_ge(bar, l * (4 * NBAR) + 4 * 6)
                        sp.dma_start(SK[:, :, :], subk[l]).then_inc(l_in, 16)
                    load(l, B_WQ + n, WR[:, (B_WQ + n) % RING, 0:D], wq[l, n])

                def load_u(i, step, n):
                    sp.wait_ge(u_split, l * E1 + i * step + (n + 1))
                    sp.dma_start(WR[:, n % 2, 0:D], uT[l, i * step + n]).then_inc(u_in[n % 2], 16)

                def load_v(i, m, tile):
                    sp.wait_ge(v_split, l * E1 + i * 4 + (m + 1))
                    sp.dma_start(WR[:, 2 + m % 2, 0:D], vtab[l, i * 4 + tile]).then_inc(v_in[m % 2], 16)

                def pair(rows, i, k, tile):
                    return rows[bass.ds(i * 4 + (tile + k), 2)].rearrange("a b t -> b a t")

                sp.wait_ge(w_used, l * BLOCKS + (BLOCKS + RING))
                for n in range(2):
                    load_u(0, 0, n)
                with sp.Fori(0, EARLY // 2) as i:
                    for k in range(2):
                        load_u(i, 2, k + 2)

                def late(i, first, last):
                    for k in range(4):
                        if not last or k < 2:
                            load_u(i, 4, first + EARLY + k + 2)
                        if k == 0:
                            sp.wait_ge(bar, l * (4 * NBAR) + 4 * 8)
                        if k % 2 == 0:
                            sp.wait_ge(o_ready, l * (4 * E1) + i * 16 + (4 * first + 4 * k + 8))
                            sp.dma_start(GT[:, k:k + 2, :], pair(gates, i, k, first + EARLY)).then_inc(g_in[k // 2], 16)
                        load_v(i, first + k, first + EARLY + k)

                with sp.Fori(0, LATE // 4 - 1) as i:
                    late(i, 0, False)
                late(0, LATE - 4, True)
                with sp.Fori(0, EARLY // 4) as i:
                    for k in range(4):
                        if k % 2 == 0:
                            sp.wait_ge(h_ready, l * E1 + i * 4 + (LATE + k + 2))
                            sp.dma_start(GT[:, k:k + 2, :], pair(gates, i, k, 0)).then_inc(g_in[k // 2], 16)
                            sp.dma_start(HW[:, k:k + 2, :], pair(early_rows, i, k, 0)).then_inc(a_in[k // 2], 16)
                        load_v(i, LATE + k, k)
            sp.wait_ge(layer_free, DEPTH + 1)
            sp.dma_start(yT, XT[:, :, :]).then_inc(y_out, 16)
            sp.wait_ge(y_out, 16)
            sp.wait_ge(st_out, 48 * DEPTH)

        @block.tensor
        def _(pe):
            for _ in range(RING):
                pe.nop().then_inc(w_used, 1)
            for _ in range(2):
                pe.nop().then_inc(u_used, 1)
            for _ in range(16):
                pe.nop().then_inc(o_ready, 1)
            for _ in range(2):
                pe.nop().then_inc(gmm_done, 1)

            def both(out, lhsT, rhs, start, stop, n=TOK):
                pe.matmul(out(0, 512), lhsT, rhs(0, 512), start=start, stop=stop)
                return pe.matmul(out(512, n), lhsT, rhs(512, n), start=start, stop=stop)

            def cols(base, parts=P):
                return lambda lo, hi: PF[0:parts, base + lo:base + hi]

            def split_product(out, part, c, start, stop, whole, spans):
                for i, (w, h) in enumerate(((0, 0), (0, 1), (1, 0))):
                    for lo, hi in spans:
                        last = pe.matmul(out(lo, hi), part(w, c), whole(h, c, lo, hi), start=start and i == 0, stop=stop and i == 2)
                return last

            def halves(l, n):
                m = SPLIT_NO[n]
                pe.wait_ge(split, l * N_SPLIT + (m + 1))
                return lambda w, c: UR[:, m % 2, w, c * P:(c + 1) * P]

            def of_h(h, c, lo, hi):
                return HR[:, h, c, lo:hi]

            TWO = ((0, 512), (512, TOK))

            def weights(l, n):
                pe.wait_ge(w_in[n % RING], l * (16 * PER_SLOT[n % RING]) + 16 * (loads(n) + 1))
                return WR[:, n % RING, :]

            def norm(l, which):
                for c in range(DC):
                    pe.wait_ge(sq_ready, l * (2 * DC) + (which * DC + c + 1))
                    last = both(cols(0), ones, lambda lo, hi: NSQ[:, c, lo:hi], c == 0, c == DC - 1)
                last.then_inc(ss_ready, 1)

            def project(l, n):
                kind, j = items[n]
                base = 1024 * (n % 2)
                if n >= 2:
                    pe.wait_ge(y_ready, l * NI + (n - 1))
                if kind == "dq":
                    w = weights(l, B_DQ)
                    if j == 0:
                        pe.wait_ge(yn_ready, l * NN + (norm_no[at_item["qa", 1]] + 1))
                        pe.wait_ge(v_out, (l + 1) * TILES)
                    for kc in range(2):
                        lhsT = w[:, kc * HEADS * D_QK + j * D_QK:kc * HEADS * D_QK + (j + 1) * D_QK]
                        last = both(cols(base, D_QK), lhsT, lambda lo, hi: QA[:, kc, lo:hi], kc == 0, kc == 1)
                    last.then_inc(w_used if j == HEADS - 1 else pj_ready, 1)
                elif kind == "dk":
                    w = weights(l, B_KV)
                    both(cols(base, D_QK), w[:, j * D_QK:(j + 1) * D_QK], lambda lo, hi: KT[:, 4, lo:hi], True, False, KEYS)
                    both(cols(base, D_QK), sel_kr, lambda lo, hi: KR[0:D_ROPE, lo:hi], False, True, KEYS).then_inc(pj_ready, 1)
                else:
                    part = halves(l, B_FM + n)
                    for c in range(DC):
                        if n == 0:
                            pe.wait_ge(hr_ready, l * (2 * DC) + (c + 1))
                        last = split_product(cols(base), part, c, c == 0, c == DC - 1, of_h, TWO)
                    last.then_inc(w_used, 1)

            def head_sums(l, n):
                kind, _ = items[n]
                if n not in norm_no:
                    return
                pe.wait_ge(y_ready, l * NI + (n + 1))
                if norm_no[n] >= 1:
                    pe.wait_ge(qstd_ready, l * NN + norm_no[n])
                parts = D_QK if kind in ("dq", "dk") else P
                group = {"aq": grp32, "ak": grp32, "bq": grp64, "bk": grp64, "cq": grp64, "ck": grp64,
                         "qa": ones, "ckv": ones}.get(kind, CN[0:D_QK, C_ONES:C_ONES + D_QK])
                if kind == "qa":
                    both(cols(2048), ones, lambda lo, hi: SQX[:, lo:hi], True, False)
                both(cols(2048, parts), group, lambda lo, hi: SQ[0:parts, n % 2, lo:hi], kind != "qa", True,
                     KEYS if kind == "dk" else TOK).then_inc(qs_ready, 1)

            def rotate(l, n):
                if n not in rope_no:
                    return
                kind, _ = items[n]
                r = rope_no[n]
                pe.wait_ge(yn_ready, l * NN + (norm_no[n] + 1))
                if r >= 1:
                    pe.wait_ge(rope_done, l * NR + r)
                parts = D_QK if kind in ("dq", "dk") else P
                m = rot32 if kind[0] == "a" else rot96 if kind[0] == "d" else rot64
                pe.matmul(bank(6, LAT, parts), m, YN[0:parts, r % 2, :], start=True, stop=True).then_inc(rot_ready, 1)

            def values(l):
                pe.wait_ge(y_ready, l * NI + N_FM)
                for n in range(N_V):
                    pe.wait_ge(split, l * N_SPLIT + (SPLIT_NO[B_V + n] + 1))
                    w = UR[:, SPLIT_NO[B_V + n] % 2]
                    for t in range(TILES):
                        for cc in range(2):
                            c = 2 * n + cc
                            for m, (h, x) in enumerate(((0, 0), (1, 0), (0, 1))):
                                last = pe.matmul(bank(t if t < 4 else 7), HR[:, h, c, qcols(t)], w[:, x, cc * 512:(cc + 1) * 512],
                                                 start=c == 0 and m == 0, stop=c == DC - 1 and m == 2)
                    last.then_inc(w_used, 1)

            def d_values(l):
                pe.wait_ge(y_ready, l * NI + NI)
                w = weights(l, B_KV)
                for t in range(KTILES):
                    last = pe.matmul(PF[:, 256 * t:256 * t + 256], KT[:, 4, qcols(t)], w[:, HEADS * D_QK:HEADS * (D_QK + HD)],
                                     start=True, stop=True)
                last.then_inc(w_used, 1)

            def scores(l, u):
                br, j, t, hh = units[u]
                h = 2 * j + hh
                for g in maps_of[u]:
                    if g >= 2:
                        pe.wait_ge(exp_done, l * NM + (g - 1))
                    if br == "A":
                        f = 2 * h + maps[g][1]
                        rows = slice(32 * (f % 4), 32 * (f % 4) + 32)
                        q, k = QT[rows, f // 4, qcols(t)], KT[rows, f // 4, :]
                    elif br == "D":
                        q, k = DQ[0:D_QK, h, qcols(t)], DK[0:D_QK, h, :]
                    else:
                        rows = slice(64 * (h // 2), 64 * (h // 2) + 64)
                        b = 2 if br == "B" else 4
                        q, k = QT[rows, b + h % 2, qcols(t)], KT[rows, 2 if br == "B" else 3, :]
                    at = 1024 * (g % 2)
                    for lo, hi in key_spans(br, t):
                        last = pe.matmul(PF[:, at:at + hi - lo], q, k[:, lo:hi], start=True, stop=True)
                        at += hi - lo
                    last.then_inc(s_ready, 1)

            def turn(l, u, modulation):
                br, j, t, hh = units[u]
                pe.wait_ge(p_ready, l * NU + (u + 1))
                if u >= 1:
                    pe.wait_ge(pt_ready, l * NU + u)
                if u % 2 == 0 and 0 <= u // 2 - 1 < N_ADA2:
                    n = u // 2 - 1
                    modulation(n // RING, n % RING, B_ADA2, MOD2[:, 2 * RING * (n // RING):2 * RING * (n // RING + 1)])
                for i in range(len(key_tiles(br, t))):
                    last = pe.transpose(PF[:, 2048 + P * i:2048 + P * i + P], PB[:, u % 3, 0, P * i:P * i + P], ident)
                last.then_inc(t_ready, 1)

            def weigh(l, u):
                br, j, t, hh = units[u]
                h = 2 * j + hh
                pe.wait_ge(pt_ready, l * NU + (u + 1))
                if hh == 0 and u >= 4:
                    pe.wait_ge(o_done, l * (NU // 2) + (u // 2 - 1))
                v = {"A": lambda kt: VT[:, kt, 64 * h:64 * h + 64],
                     "B": lambda kt: VT[:, kt, 256 + 64 * (h // 2):320 + 64 * (h // 2)],
                     "C": lambda kt: VT[:, kt, 384 + 64 * (h // 2):448 + 64 * (h // 2)],
                     "D": lambda kt: VD[:, kt, 64 * h:64 * h + 64]}[br]
                tiles = key_tiles(br, t)
                out = PF[64 * hh:64 * hh + 64, 3072 + 512 * (u // 2 % 2):3072 + 512 * (u // 2 % 2) + P]
                for i, kt in enumerate(tiles):
                    last = pe.matmul(out, v(kt), PT[:, u % 2, P * i:P * i + P], start=i == 0, stop=i == len(tiles) - 1)
                last.then_inc(pv_done, 1)

            pe.wait_ge(c_in, 32)
            pe.wait_ge(cs_ready, 1)
            with pe.Fori(0, DEPTH) as l:
                def modulation(i, k, at, out):
                    if k % 2 == 0:
                        pe.wait_ge(w_in[k], l * (16 * PER_SLOT[k]) + i * 16 + 16 * (at // RING + 1))
                    if k == 0 and at == 0:
                        pe.wait_ge(mod_copied, l * (N_ADA1 // RING) + i + 1)
                    for c in range(DC):
                        last = pe.matmul(out[:, 2 * k:2 * k + 2], WR[:, k, c * P:(c + 1) * P], CS[:, 2 * c:2 * c + 2],
                                         start=c == 0, stop=c == DC - 1)
                    last.then_inc(w_used, 1)

                norm(l, 0)
                with pe.Fori(0, N_ADA1 // RING) as i:
                    for k in range(RING):
                        modulation(i, k, 0, bank(7, 8))
                phase_end(pe, l, 0)
                for s in range(NI + 2):
                    if s == N_FM:
                        values(l)
                    if s < NI:
                        if items[s] == ("dk", 0):
                            pe.wait_ge(l_in, l * 96 + 80)
                            pe.wait_ge(yn_ready, l * NN + (norm_no[at_item["ckv", 0]] + 1))
                        project(l, s)
                    if 1 <= s <= NI:
                        head_sums(l, s - 1)
                    if s >= 2:
                        rotate(l, s - 2)
                d_values(l)
                phase_end(pe, l, 1)
                for s in range(NU + 3):
                    if s < NU:
                        scores(l, s)
                    if 2 <= s < NU + 2:
                        turn(l, s - 2, modulation)
                    if s >= 3:
                        weigh(l, s - 3)
                phase_end(pe, l, 2)
                for j in range(2):
                    pe.wait_ge(sub_sq, l * 2 + (j + 1))
                    both(cols(1024 * j), grp64, lambda lo, hi: HSQ[:, j, lo:hi], True, True).then_inc(sub_ss, 1)
                phase_end(pe, l, 3)
                with pe.Fori(0, DC) as i:
                    for k in range(4):
                        pe.wait_ge(w_in[k], l * (16 * PER_SLOT[k]) + i * 16 + 16 * (loads(B_GATE + k) + 1))
                        pe.wait_ge(gm_free, l * N_GATE + i * 4 + (k + 1))
                        pe.wait_ge(split, l * N_SPLIT + i * 4 + (SPLIT_NO[B_GATE] + k + 1))
                        for c in range(DC):
                            last = split_product(cols(1024 * (k % 2)), lambda w, c: UR[:, (SPLIT_NO[B_GATE] + k) % 2, w, c * P:(c + 1) * P],
                                                 c, c == 0, c == DC - 1, of_h, TWO)
                        last.then_inc(g_ready, 1)
                        for e in range(2):
                            last = both(cols(2048 + 1024 * (k % 2)), WR[:, k, D + e * P:D + (e + 1) * P],
                                        lambda lo, hi: OUT[:, 2 * k + e, lo:hi], e == 0, e == 1)
                        last.then_inc(w_used, 1)
                pe.wait_ge(gm_free, l * N_GATE + (N_GATE + 2))
                for n in range(N_WOUT):
                    w = weights(l, B_WOUT + n)
                    if n >= 2:
                        pe.wait_ge(wo_done, l * N_WOUT + (n - 1))
                    for c in range(DC):
                        last = both(cols(1024 * (n % 2)), w[:, c * P:(c + 1) * P], lambda lo, hi: YS[:, c, lo:hi],
                                    c == 0, c == DC - 1)
                    last.then_inc(w_used, 1)
                phase_end(pe, l, 4)
                norm(l, 1)
                phase_end(pe, l, 5)
                for n in range(N_WQ):
                    part = halves(l, B_WQ + n)
                    if n >= 4:
                        pe.wait_ge(q_done, l * N_WQ + (n - 3))
                    for c in range(DC):
                        if n == 0:
                            pe.wait_ge(hr_ready, l * (2 * DC) + (DC + c + 1))
                        last = split_product(cols(1024 * (n % 4)), part, c, c == 0, c == DC - 1, of_h, TWO)
                    last.then_inc(w_used, 1)
                pe.wait_ge(q_done, l * N_WQ + N_WQ)
                pe.wait_ge(l_in, l * 96 + 96)

                for t in range(TILES):
                    if t >= 1:
                        pe.wait_ge(s_evac, l * TILES + t)
                    for b in range(SUB):
                        last = pe.matmul(PF[:, P * b:P * b + P], PQ[:, b, qcols(t)], SK[:, b, :], start=True, stop=True)
                    last.then_inc(sc_ready, 1)
                phase_end(pe, l, 6)

                def u_chunk(i, step, n, c):
                    if c == 0:
                        pe.wait_ge(u_split, l * E1 + i * step + (n + 3))
                        pe.wait_ge(ge_done, l * E1 + i * step + (n + 1))
                    last = split_product(cols(1024 * (n % 2)), lambda w, c: UR[:, n % 2, w, c * P:(c + 1) * P],
                                         c, c == 0, c == DC - 1, of_h, TWO)
                    if c == DC - 1:
                        last.then_inc(u_used, 1)

                for t in range(TILES):
                    with pe.Fori(0, AHEAD // 2 - 1) as i:
                        for k in range(2):
                            for c in range(DC):
                                u_chunk(i, 2, PER_TILE * t + k, c)
                    for c in range(DC):
                        u_chunk(0, 0, PER_TILE * t + AHEAD - 2, c)
                    pe.wait_ge(tk_ready, l * TILES + (t + 1))
                    for i in range(3):
                        last = pe.transpose(PF[:, 2048 + P * i:2048 + P * i + P], EW[:, i, :], ident)
                    last.then_inc(tr_ready, 1)
                    for c in range(DC):
                        u_chunk(0, 0, PER_TILE * t + AHEAD - 1, c)
                    with pe.Fori(0, 2) as i:
                        for m in range(BATCHES):
                            b = m % 2
                            pe.wait_ge(hot_ready, l * (32 * TILES) + i * BATCHES + (32 * t + m + 1))
                            pe.wait_ge(g_evac, l * (32 * TILES) + i * BATCHES + (32 * t + m + 1))
                            for k in range(4):
                                last = pe.matmul(bank(5 + b)[:, P * k:P * k + P], HOT[:, b, 2 * k, :], HOT[:, b, 2 * k + 1, :],
                                                 start=True, stop=True)
                            last.then_inc(gmm_done, 1)
                            u_chunk(i, 2, PER_TILE * t + AHEAD + m // DC, m % DC)
                for n in range(EARLY - AFTER, EARLY):
                    for c in range(DC):
                        u_chunk(0, 0, n, c)
                phase_end(pe, l, 7)

                def v_half(i, m):
                    pe.wait_ge(v_split, l * E1 + i * 4 + (m + 4))
                    pe.wait_ge(h_ready, l * E1 + i * 4 + (m + 6))
                    for d in range(DC):
                        pe.wait_ge(ac_done, l * (4 * E1) + i * 16 + (4 * m + d + 1))
                        for k in range(2):
                            e = (m + k) % 4
                            last = split_product(cols(2048 + 1024 * (d % 2)), lambda w, c: VR[:, e, w, c * P:(c + 1) * P], d,
                                                 k == 0, k == 1, lambda h, c, lo, hi: HB[:, e, h, lo:hi], TWO)
                        last.then_inc(o_ready, 1)

                with pe.Fori(0, LATE // 4) as i:
                    for k in range(4):
                        for c in range(DC):
                            u_chunk(i, 4, EARLY + k, c)
                    for m in (0, 2):
                        v_half(i, m)
                with pe.Fori(0, EARLY // 4) as i:
                    for m in (0, 2):
                        v_half(i, LATE + m)
                phase_end(pe, l, 8)

        @block.scalar
        def _(act):
            for _ in range(2):
                act.nop().then_inc(ge_done, 1)
                act.nop().then_inc(g_evac, 1)
            for k in range(2):
                act.nop().then_inc(a_out[k], 16)
            act.wait_ge(c_in, 32)
            nc.scalar.activation(SM[:, 144:160], CS[:, :], ACT.Sigmoid).then_inc(cs_sig, 1)
            act.wait_ge(x_in, 16)

            def norm(l, which):
                for c in range(DC):
                    nc.scalar.activation(NSQ[:, c, :], XT[:, c, :], ACT.Square).then_inc(sq_ready, 1)
                act.wait_ge(ss_ready, l * 2 + (which + 1))
                nc.scalar.activation(NSTD, PF[:, 0:TOK], ACT.Sqrt, bias=eps, scale=1.0 / D).then_inc(std_ready, 1)

            def high_h(l, which):
                for c in range(DC + 1):
                    if c < DC:
                        act.wait_ge(ht_ready, l * (2 * DC) + (which * DC + c + 1))
                        for g, span in enumerate((slice(0, LAT), slice(LAT, TOK))):
                            last = nc.scalar.activation(HT[:, c, span], HT[:, c, span], ACT.Identity, bias=MD4[:, 3 * which, c, g:g + 1],
                                                        scale=1.0)
                        last.then_inc(hs_ready, 1)
                    if c >= 1:
                        act.wait_ge(hs_ready, l * (2 * DC) + (which * DC + c))
                        nc.scalar.copy(HR[:, 0, c - 1, :], HT[:, c - 1, :]).then_inc(hh_ready, 1)

            def used(l, n):
                act.wait_ge(w_used, l * BLOCKS + (RING + n + 1))

            def raw(l, n):
                kind, j = items[n]
                base = 1024 * (n % 2)
                if n < N_FM or (kind, j) == ("dq", HEADS - 1):
                    used(l, B_FM + n if n < N_FM else B_DQ)
                else:
                    act.wait_ge(pj_ready, l * (2 * HEADS - 1) + (j + 1 if kind == "dq" else HEADS + j))
                if kind == "kr":
                    nc.scalar.copy(KR[0:D_ROPE, 0:LAT], PF[0:D_ROPE, base:base + LAT])
                    nc.scalar.copy(KR[0:D_ROPE, NEWK:KEYS], PF[0:D_ROPE, base + LAT:base + TOK]).then_inc(y_ready, 1)
                    return
                if (kind, j) == ("qa", 0):
                    nc.scalar.copy(QA[:, 0, :], PF[:, base:base + TOK])
                    nc.scalar.activation(SQX, PF[:, base:base + TOK], ACT.Square).then_inc(y_ready, 1)
                    return
                before = [m for m in norm_no if m <= n - 2]
                if before:
                    act.wait_ge(yn_ready, l * NN + (norm_no[before[-1]] + 1))
                parts, w = (D_QK if kind in ("dq", "dk") else P), (KEYS if kind == "dk" else TOK)
                nc.scalar.copy(YB[0:parts, n % 2, 0:w], PF[0:parts, base:base + w])
                nc.scalar.activation(SQ[0:parts, n % 2, 0:w], PF[0:parts, base:base + w], ACT.Square).then_inc(y_ready, 1)

            def std(l, n):
                if n not in norm_no:
                    return
                kind, _ = items[n]
                act.wait_ge(qs_ready, l * NN + (norm_no[n] + 1))
                parts, w = (D_QK if kind in ("dq", "dk") else P), (KEYS if kind == "dk" else TOK)
                size = {"a": A_QK, "b": HD, "c": HD, "d": D_QK}[kind[0]] if kind not in ("qa", "ckv") else \
                    {"qa": 256, "ckv": 128}[kind]
                size = {"qa": 256, "ckv": 128}.get(kind, size)
                nc.scalar.activation(STD[0:parts, n % 2, 0:w], PF[0:parts, 2048:2048 + w], ACT.Sqrt, bias=eps[0:parts],
                                     scale=1.0 / size).then_inc(qstd_ready, 1)

            def exps(l, u):
                br, j, t, hh = units[u]
                if u >= 3:
                    act.wait_ge(t_ready, l * NU + (u - 2))
                for g in maps_of[u]:
                    s = slice(g % 8, g % 8 + 1)
                    act.wait_ge(nm_ready, l * NM + (g + 1))
                    if br == "B":
                        sink = GN[:, G_SINK + 2 * j + hh:G_SINK + 2 * j + hh + 1]
                        nc.scalar.activation(ES[:, s], sink, ACT.Exp, bias=NM_[:, s], scale=1.0)
                    n = P * len(key_tiles(br, t))
                    nc.scalar.activation(PB[:, u % 3, maps[g][1], 0:n], PF[:, 1024 * (g % 2):1024 * (g % 2) + n], ACT.Exp,
                                         bias=NM_[:, s], scale=SCALE[br], accum_out=SU[:, s]).then_inc(exp_done, 1)

            def turned(l, u):
                br, j, t, hh = units[u]
                act.wait_ge(t_ready, l * NU + (u + 1))
                if u >= 2:
                    act.wait_ge(pv_done, l * NU + (u - 1))
                n = P * len(key_tiles(br, t))
                nc.scalar.copy(PT[:, u % 2, 0:n], PF[:, 2048:2048 + n]).then_inc(pt_ready, 1)

            def heads(l, g):
                br, j, t, _ = units[2 * g]
                act.wait_ge(pv_done, l * NU + (2 * g + 2))
                nc.scalar.copy(OUT[:, 2 * "ABCD".index(br) + j, qcols(t)], bank(6 + g % 2, P)).then_inc(o_done, 1)

            def sigmoid(l, i, k):
                act.wait_ge(g_ready, l * N_GATE + i * 4 + (k + 1))
                act.wait_ge(gm_free, l * N_GATE + i * 4 + (k + 1))
                nc.scalar.activation(SG[:, k % 2, :], PF[:, 1024 * (k % 2):1024 * (k % 2) + TOK], ACT.Sigmoid).then_inc(sg_ready, 1)

            def high(l, n):
                m = SPLIT_NO[n]
                act.wait_ge(w_in[n % RING], l * (16 * PER_SLOT[n % RING]) + 16 * (loads(n) + 1))
                before = [x for x in SPLIT_NO if SPLIT_NO[x] == m - 2]
                if before:
                    used(l, before[0])
                nc.scalar.copy(UR[:, m % 2, 0, :], WR[:, n % RING, 0:D]).then_inc(hi_ready, 1)

            with act.Fori(0, DEPTH) as l:
                norm(l, 0)
                act.wait_ge(lam_sum, l + 1)
                nc.scalar.activation(LAME, LAMS, ACT.Exp).then_inc(lam_exp, 1)
                high(l, B_FM)
                high(l, B_FM + 1)
                phase_end(act, l, 0)
                high_h(l, 0)
                for s in range(NI + 1):
                    if s < N_FM:
                        high(l, B_FM + s + 2)
                    if s == N_FM:
                        for n in range(2, N_V):
                            high(l, B_V + n)
                        used(l, B_V + N_V - 1)
                        for t in range(TILES):
                            nc.scalar.copy(VT[:, t if t < 4 else 5, :], bank(t if t < 4 else 7)).then_inc(v_out, 1)
                    if s < NI:
                        raw(l, s)
                    if s >= 1:
                        std(l, s - 1)
                used(l, B_KV)
                act.wait_ge(yn_ready, (l + 1) * NN)
                nc.scalar.copy(VD.rearrange("p a b -> p (a b)"), PF[:, 0:256 * KTILES])
                phase_end(act, l, 1)
                act.dma_start(st_k[l], KT[:, :, NEWK:KEYS]).then_inc(st_out, 16)
                act.dma_start(st_kr[l], KR[0:D_ROPE, NEWK:KEYS]).then_inc(st_out, 16)
                act.dma_start(st_v[l], VT[:, 5, :]).then_inc(st_out, 16)
                for s in range(NU + 4):
                    if s < NU:
                        exps(l, s)
                    if 2 <= s < NU + 2:
                        turned(l, s - 2)
                    if s >= 4 and (s - 4) % 2 == 1:
                        heads(l, (s - 4) // 2)
                def high_gate(i, k):
                    m = SPLIT_NO[B_GATE] + k
                    act.wait_ge(w_in[k % 4], l * (16 * PER_SLOT[k % 4]) + i * 16 + 16 * (loads(B_GATE + k) + 1))
                    if k >= 2:
                        act.wait_ge(g_ready, l * N_GATE + i * 4 + (k - 1))
                    nc.scalar.copy(UR[:, m % 2, 0, :], WR[:, k % 4, 0:D]).then_inc(hi_ready, 1)

                for k in range(2):
                    high_gate(0, k)
                phase_end(act, l, 2)
                for j in range(2):
                    nc.scalar.activation(HSQ[:, j, :], OUT[:, j, :], ACT.Square).then_inc(sub_sq, 1)
                for j in range(2):
                    act.wait_ge(sub_ss, l * 2 + (j + 1))
                    nc.scalar.activation(HSTD[:, j, :], PF[:, 1024 * j:1024 * j + TOK], ACT.Sqrt, bias=eps,
                                         scale=1.0 / HD).then_inc(sub_std, 1)
                act.wait_ge(st_out, l * 48 + 48)
                settled(act)
                phase_end(act, l, 3)

                with act.Fori(0, DC - 1) as i:
                    for k in range(4):
                        high_gate(i, k + 2)
                        sigmoid(l, i, k)
                for k in range(4):
                    if k < 2:
                        high_gate(DC - 1, k + 2)
                    sigmoid(l, DC - 1, k)
                for n in range(2):
                    high(l, B_WQ + n)
                phase_end(act, l, 4)
                norm(l, 1)
                phase_end(act, l, 5)
                high_h(l, 1)
                for n in range(N_WQ):
                    used(l, B_WQ + n)
                    if n + 2 < N_WQ:
                        high(l, B_WQ + n + 2)
                    nc.scalar.copy(PQ[:, n, :], PF[:, 1024 * (n % 4):1024 * (n % 4) + TOK]).then_inc(q_done, 1)

                def high_u(i, step, n):
                    act.wait_ge(u_in[n % 2], l * (8 * E1) + i * (8 * step) + 16 * (n // 2 + 1))
                    act.wait_ge(u_used, l * E1 + i * step + (n + 1))
                    nc.scalar.copy(UR[:, n % 2, 0, :], WR[:, n % 2, 0:D]).then_inc(uh_ready, 1)

                def gelu(dst, i, step, n):
                    act.wait_ge(u_used, l * E1 + i * step + (n + 3))
                    nc.scalar.activation(dst, PF[:, 1024 * (n % 2):1024 * (n % 2) + TOK], ACT.Gelu).then_inc(ge_done, 1)

                def early(i, n):
                    high_u(i, 2, n + 2)
                    act.wait_ge(a_out[n % 2], l * (8 * EARLY) + i * 16 + 16 * (n // 2 + 1))
                    gelu(AS[:, n % 2, :], i, 2, n)
                    act.wait_ge(ge_done, l * E1 + i * 2 + (n + 3))
                    act.dma_start(early_rows[i * 2 + n], AS[:, n % 2, :]).then_inc(a_out[n % 2], 16)

                high_u(0, 0, 0)
                high_u(0, 0, 1)
                for t in range(TILES):
                    act.wait_ge(sc_ready, l * TILES + (t + 1))
                    if t >= 2:
                        act.wait_ge(ss_out[t % 2], l * (16 * tiles_of(t % 2)) + 16 * (t // 2))
                    nc.scalar.copy(SS[:, t % 2, :], PF[:, 0:2048]).then_inc(s_evac, 1)
                    act.wait_ge(s_evac, l * TILES + (t + 1))
                    act.dma_start(sub_rows[t], SS[:, t % 2, :]).then_inc(ss_out[t % 2], 16)
                for k in range(2):
                    act.wait_ge(ss_out[k], (l + 1) * (16 * tiles_of(k)))
                    settled(act)
                phase_end(act, l, 6)
                act.dma_start(S1, sub_rows[0]).then_inc(ss_in, 16)
                for t in range(TILES):
                    n0 = PER_TILE * t
                    with act.Fori(0, AHEAD // 2 - 2) as i:
                        for k in range(2):
                            early(i, n0 + k)
                    act.wait_ge(cm_ready, l * TILES + (t + 1))
                    nc.scalar.activation(CE, CM, ACT.Exp).then_inc(ce_ready, 1)
                    for k in range(AHEAD - 4, AHEAD - 1):
                        early(0, n0 + k)
                    act.wait_ge(tr_ready, l * TILES + (t + 1))
                    nc.scalar.copy(EWT.rearrange("p a b -> p (a b)"), PF[:, 2048:2048 + 3 * P]).then_inc(ewt_ready, 1)
                    if t + 1 < TILES:
                        act.dma_start(S1, sub_rows[t + 1]).then_inc(ss_in, 16)
                    early(0, n0 + AHEAD - 1)
                    if t >= 1:
                        act.wait_ge(gd_out, l * (16 * TILES) + 16 * t)
                    with act.Fori(0, 2) as i:
                        for m in range(BATCHES):
                            act.wait_ge(gmm_done, l * (32 * TILES) + i * BATCHES + (32 * t + m + 3))
                            nc.scalar.copy(GB[:, :, bass.ds(i * HALF + 4 * m, 4)],
                                           bank(5 + m % 2).rearrange("p (t e) -> p e t", t=4)).then_inc(g_evac, 1)
                            if m % DC == DC - 1:
                                early(i, n0 + AHEAD + m // DC)
                    act.wait_ge(g_evac, l * (32 * TILES) + (32 * (t + 1) + 2))
                    act.dma_start(gates[:, :, qcols(t)].rearrange("a b t -> b a t"), GB[:, :, :]).then_inc(gd_out, 16)
                for n in range(EARLY - AFTER, EARLY):
                    early(0, n)
                act.wait_ge(gd_out, l * (16 * TILES) + 16 * TILES)
                settled(act)
                for k in range(2):
                    act.wait_ge(a_out[k], (l + 1) * (8 * EARLY) + 16)
                    settled(act)
                phase_end(act, l, 7)

                def high_v(i, m):
                    act.wait_ge(v_in[m % 2], l * (8 * E1) + i * 32 + 16 * (m // 2 + 1))
                    if m % 2 == 0:
                        act.wait_ge(o_ready, l * (4 * E1) + i * 16 + (4 * m + 8))
                    nc.scalar.copy(VR[:, m % 4, 0, :], WR[:, 2 + m % 2, 0:D]).then_inc(vh_ready, 1)

                def late(i, first, last):
                    for k in range(4):
                        if not last or k < 2:
                            high_u(i, 4, first + EARLY + k + 2)
                        act.wait_ge(h_ready, l * E1 + i * 4 + (first + k + 1))
                        gelu(HW[:, k, :], i, 4, first + EARLY + k)
                        high_v(i, first + k)

                with act.Fori(0, LATE // 4 - 1) as i:
                    late(i, 0, False)
                late(0, LATE - 4, True)
                with act.Fori(0, EARLY // 4) as i:
                    for k in range(4):
                        high_v(i, LATE + k)
                phase_end(act, l, 8)

        @block.vector
        def _(dve):
            dve.nop().then_inc(mod_copied, 1)
            for _ in range(4):
                dve.nop().then_inc(h_ready, 1)
            dve.nop().then_inc(layer_free, 1)
            for _ in range(2):
                dve.nop().then_inc(gm_free, 1)
                dve.nop().then_inc(ac_done, 1)
            dve.wait_ge(c_in, 32)
            dve.wait_ge(cs_sig, 1)
            nc.vector.tensor_tensor(CS[:, :], CS[:, :], SM[:, 144:160], ALU.mult).then_inc(cs_ready, 1)
            dve.wait_ge(x_in, 16)

            def norm(l, which):
                dve.wait_ge(std_ready, l * 2 + (which + 1))
                nc.vector.reciprocal(NRS, NSTD)
                dve.drain()

            def scaled(l, which):
                for c in range(DC):
                    for g, span in enumerate((slice(0, LAT), slice(LAT, TOK))):
                        last = nc.vector.scalar_tensor_tensor(HT[:, c, span], XT[:, c, span], SC[:, which, c, g:g + 1], NRS[:, span],
                                                              ALU.mult, ALU.mult)
                    last.then_inc(ht_ready, 1)

            def target(kind, j):
                return {"aq": lambda: QT[:, j, :], "bq": lambda: QT[:, 2 + j, :], "cq": lambda: QT[:, 4 + j, :],
                        "ak": lambda: KT[:, j, :], "bk": lambda: KT[:, 2, :], "ck": lambda: KT[:, 3, :],
                        "ckv": lambda: KT[:, 4, :], "qa": lambda: QA[:, j, :],
                        "dq": lambda: DQ[0:D_QK, j, :], "dk": lambda: DK[0:D_QK, j, :]}[kind]()

            def head_norm(l, n):
                if n not in norm_no:
                    return
                kind, j = items[n]
                parts, w = (D_QK if kind in ("dq", "dk") else P), (KEYS if kind == "dk" else TOK)
                gcol = {"aq": G_AQ, "ak": G_AK, "bq": G_BQ, "bk": G_BK, "cq": G_CQ, "ck": G_CK, "qa": G_QA + 1,
                        "ckv": G_CKV, "dq": G_DQ, "dk": G_DK}[kind]
                gain = GN[0:parts, gcol:gcol + 1]
                dest = target(kind, j)
                dve.wait_ge(qstd_ready, l * NN + (norm_no[n] + 1))
                nc.vector.reciprocal(RST[0:parts, 0:w], STD[0:parts, n % 2, 0:w])
                dve.drain()
                if kind == "qa":
                    nc.vector.scalar_tensor_tensor(QA[:, 0, :], QA[:, 0, :], GN[:, G_QA:G_QA + 1], RST[:, 0:TOK], ALU.mult, ALU.mult)
                lat = YN[0:parts, rope_no[n] % 2, :] if n in rope_no else dest[:, 0:LAT]
                nc.vector.scalar_tensor_tensor(lat, YB[0:parts, n % 2, 0:LAT], gain, RST[0:parts, 0:LAT], ALU.mult, ALU.mult)
                rest = dest[:, NEWK:KEYS] if kind in ("ak", "bk", "ck", "ckv") else dest[:, LAT:w]
                nc.vector.scalar_tensor_tensor(rest, YB[0:parts, n % 2, LAT:w], gain, RST[0:parts, LAT:w], ALU.mult, ALU.mult)
                dve.drain().then_inc(yn_ready, 1)

            def rope(l, n):
                if n not in rope_no:
                    return
                kind, j = items[n]
                r = rope_no[n]
                parts = D_QK if kind in ("dq", "dk") else P
                tab = {"a": 0, "b": 1, "c": 1, "d": 2}[kind[0]]
                dve.wait_ge(rot_ready, l * NR + (r + 1))
                nc.vector.tensor_tensor(T2[0:parts, :], bank(6, LAT, parts), TG[0:parts, 2 * tab + 1, :], ALU.mult)
                dve.drain()
                dve.wait_ge(t1_ready, l * NR + (r + 1))
                nc.vector.tensor_tensor(target(kind, j)[:, 0:LAT], T1[0:parts, r % 2, :], T2[0:parts, :], ALU.add).then_inc(rope_done, 1)
                dve.drain()

            def maxima(l, u):
                br, j, t, hh = units[u]
                for g in maps_of[u]:
                    s = slice(g % 8, g % 8 + 1)
                    n = P * len(key_tiles(br, t))
                    at = 1024 * (g % 2)
                    dve.wait_ge(s_ready, l * NM + (g + 1))
                    if br == "B" and t < 4:
                        if t > 0:
                            z = PF[:, at + P:at + 2 * P]
                            nc.vector.tensor_tensor(z, z, band["prev"], ALU.add)
                        if t < 3:
                            z = PF[:, at + n - P:at + n]
                            nc.vector.tensor_tensor(z, z, band["next"], ALU.add)
                        dve.drain()
                    nc.vector.reduce_max(MX[:, s], PF[:, at:at + n], AX.X)
                    dve.drain()
                    if br == "B":
                        sink = GN[:, G_SINK + 2 * j + hh:G_SINK + 2 * j + hh + 1]
                        nc.vector.tensor_scalar(MX[:, s], MX[:, s], SCALE[br], sink, ALU.mult, ALU.max)
                        dve.drain()
                        nc.vector.tensor_scalar(NM_[:, s], MX[:, s], -1.0, None, ALU.mult).then_inc(nm_ready, 1)
                    else:
                        nc.vector.tensor_scalar(NM_[:, s], MX[:, s], -SCALE[br], None, ALU.mult).then_inc(nm_ready, 1)

            def normalise(l, u):
                br, j, t, hh = units[u]
                gs = maps_of[u]
                n = P * len(key_tiles(br, t))
                dve.wait_ge(exp_done, l * NM + (gs[-1] + 1))
                s = slice(gs[0] % 8, gs[0] % 8 + len(gs))
                if br == "B":
                    nc.vector.tensor_tensor(SU[:, s], SU[:, s], ES[:, s], ALU.add)
                    dve.drain()
                nc.vector.reciprocal(RC[:, s], SU[:, s])
                dve.drain()
                p0, p1 = PB[:, u % 3, 0, 0:n], PB[:, u % 3, 1, 0:n]
                if br != "A":
                    nc.vector.tensor_scalar(p0, p0, RC[:, s], None, ALU.mult).then_inc(p_ready, 1)
                    return
                r0, r1 = RC[:, gs[0] % 8:gs[0] % 8 + 1], RC[:, gs[1] % 8:gs[1] % 8 + 1]
                nc.vector.tensor_tensor(r1, r1, NLAM, ALU.mult)
                nc.vector.tensor_scalar(p0, p0, r0, None, ALU.mult)
                dve.drain()
                nc.vector.scalar_tensor_tensor(p0, p1, r1, p0, ALU.mult, ALU.add).then_inc(p_ready, 1)

            def top16(values, indices, scores, spare, n):
                for b in range(n):
                    nc.vector.max(values(b)[:, 0:8], scores(b))
                dve.drain()
                for b in range(n):
                    nc.vector.max_index(indices(b)[:, 0:8], values(b)[:, 0:8], scores(b))
                    nc.vector.match_replace(spare(b), values(b)[:, 0:8], scores(b), LOWEST)
                dve.drain()
                for b in range(n):
                    nc.vector.max(values(b)[:, 8:16], spare(b))
                dve.drain()
                for b in range(n):
                    nc.vector.max_index(indices(b)[:, 8:16], values(b)[:, 8:16], spare(b))
                dve.drain()

            with dve.Fori(0, DEPTH) as l:
                dve.wait_ge(l_in, l * 96 + 16)
                lam = GN[:, G_LAM:G_LAM + 4 * A_QK].rearrange("p (i s k) -> p i s k", i=2, s=2)
                lamp = LAMP.rearrange("p (i k) -> p i k", i=2)
                nc.vector.tensor_tensor(lamp, lam[:, :, 0, :], lam[:, :, 1, :], ALU.mult)
                nc.vector.tensor_tensor(GSUB, GN[:, G_SUB:G_SUB + 1], GN[:, G_LREST:G_LREST + 1], ALU.mult)
                dve.drain()
                nc.vector.reduce_sum(LAMS, lamp, AX.X).then_inc(lam_sum, 1)
                dve.wait_ge(lam_exp, l + 1)
                nc.vector.tensor_tensor(NLAM, LAME[:, 1:2], LAME[:, 0:1], ALU.subtract)
                dve.drain()
                nc.vector.tensor_tensor(NLAM, NLAM, GN[:, G_LINIT:G_LINIT + 1], ALU.subtract)
                with dve.Fori(0, N_ADA1 // RING) as i:
                    dve.wait_ge(w_used, l * BLOCKS + i * RING + 2 * RING)
                    nc.vector.tensor_copy(MD[:, bass.ds(i * 8, 8)], bank(7, 8)).then_inc(mod_copied, 1)

                def finish_modulation(lo, hi, which, gcol):
                    dve.drain()
                    nc.vector.tensor_tensor(MD[:, lo:hi], MD[:, lo:hi], GN[:, G_ADAB + lo:G_ADAB + hi], ALU.add)
                    dve.drain()
                    gain = GN[:, gcol:gcol + 16].rearrange("p (c g) -> p c g", c=DC)
                    nc.vector.scalar_tensor_tensor(SC[:, which], MD4[:, 3 * which + 1], 1.0, gain, ALU.add, ALU.mult)

                finish_modulation(0, 2 * N_ADA1, 0, G_N1)
                dve.drain()
                norm(l, 0)
                phase_end(dve, l, 0)
                scaled(l, 0)
                dve.wait_ge(l_in, l * 96 + 80)
                for s in range(1, NI + 2):
                    if s <= NI:
                        head_norm(l, s - 1)
                    if s >= 2:
                        rope(l, s - 2)
                phase_end(dve, l, 1)
                for s in range(NU + 1):
                    if s < NU:
                        maxima(l, s)
                    if s >= 1:
                        normalise(l, s - 1)
                phase_end(dve, l, 2)
                nc.vector.tensor_copy(MD[:, 2 * N_ADA1:2 * N_ADA], MOD2)
                finish_modulation(2 * N_ADA1, 2 * N_ADA, 1, G_N2)
                for j in range(2):
                    dve.wait_ge(sub_std, l * 2 + (j + 1))
                    nc.vector.reciprocal(HRS[:, j, :], HSTD[:, j, :])
                    dve.drain()
                    nc.vector.scalar_tensor_tensor(OUT[:, j, :], OUT[:, j, :], GSUB, HRS[:, j, :], ALU.mult, ALU.mult)
                phase_end(dve, l, 3)
                with dve.Fori(0, DC) as i:
                    for k in range(4):
                        dve.wait_ge(sg_ready, l * N_GATE + i * 4 + (k + 1))
                        dve.wait_ge(w_used, l * BLOCKS + i * 4 + (RING + B_GATE + k + 1))
                        br = PF[:, 2048 + 1024 * (k % 2):2048 + 1024 * (k % 2) + TOK]
                        if k == 0:
                            nc.vector.tensor_tensor(YS[:, i, :], SG[:, 0, :], br, ALU.mult).then_inc(gm_free, 1)
                        else:
                            nc.vector.tensor_tensor(GM[:, k % 2, :], SG[:, k % 2, :], br, ALU.mult)
                            dve.drain()
                            nc.vector.tensor_tensor(YS[:, i, :], YS[:, i, :], GM[:, k % 2, :], ALU.add).then_inc(gm_free, 1)
                for n in range(N_WOUT):
                    dve.wait_ge(w_used, l * BLOCKS + (RING + B_WOUT + n + 1))
                    for g, (lo, hi) in enumerate(((0, LAT), (LAT, TOK))):
                        last = nc.vector.scalar_tensor_tensor(XT[:, n, lo:hi], PF[:, 1024 * (n % 2) + lo:1024 * (n % 2) + hi],
                                                              MD4[:, 2, n, g:g + 1], XT[:, n, lo:hi], ALU.mult, ALU.add)
                    last.then_inc(wo_done, 1)
                phase_end(dve, l, 4)
                norm(l, 1)
                phase_end(dve, l, 5)
                scaled(l, 1)
                phase_end(dve, l, 6)
                I1U, CIU, CAU, CBU = (x.bitcast(U32) for x in (I1, CI, CA, CB))
                s1, s2 = (x.rearrange("p (b k) -> p b k", b=SUB) for x in (S1, S2))
                c1, c2 = (x.rearrange("p (h k) -> p h k", h=PH) for x in (S1, S2))
                m1, m2 = (x.rearrange("p (h s k) -> p h s k", h=PH, s=TOPK) for x in (S1, S2))
                V4 = V1.rearrange("p (h s) k -> p h s k", s=2)
                F4 = I1F.rearrange("p (h s) k -> p h s k", s=2)
                all4 = [P, PH, TOPK, TOPK]
                for t in range(TILES):
                    dve.wait_ge(ss_in, l * (16 * TILES) + 16 * (t + 1))
                    settled(dve)
                    top16(lambda b: V1[:, b, :], lambda b: I1U[:, b, :], lambda b: s1[:, b, :], lambda b: s2[:, b, :], SUB)
                    nc.vector.tensor_copy(I1F, I1U)
                    nc.vector.tensor_tensor(m1, V4[:, :, 0, :].unsqueeze(3).broadcast_to(all4),
                                            V4[:, :, 1, :].unsqueeze(2).broadcast_to(all4), ALU.add)
                    dve.drain()
                    top16(lambda h: CV[:, h, :], lambda h: CIU[:, h, :], lambda h: c1[:, h, :], lambda h: c2[:, h, :], PH)
                    nc.vector.tensor_tensor(CM, CV, CV[:, :, 0:1].broadcast_to([P, PH, TOPK]), ALU.subtract).then_inc(cm_ready, 1)
                    nc.vector.tensor_single_scalar(CAU, CIU, 4, ALU.logical_shift_right)
                    nc.vector.tensor_single_scalar(CBU, CIU, 15, ALU.bitwise_and)
                    dve.drain()
                    nc.vector.tensor_copy(CAF, CAU)
                    nc.vector.tensor_copy(CBF, CBU)
                    dve.drain()
                    for side, place in enumerate((CAF, CBF)):
                        nc.vector.tensor_tensor(m1, place.unsqueeze(3).broadcast_to(all4),
                                                iota16.unsqueeze(1).unsqueeze(1).broadcast_to(all4), ALU.is_equal)
                        dve.drain()
                        nc.vector.tensor_tensor(m2, m1, F4[:, :, side, :].unsqueeze(2).broadcast_to(all4), ALU.mult)
                        dve.drain()
                        nc.vector.reduce_sum(EW[:, side, :].rearrange("p (h k) -> p h k", h=PH), m2, AX.X)
                        dve.drain()
                    dve.wait_ge(ce_ready, l * TILES + (t + 1))
                    nc.vector.reduce_sum(CSUM, CE, AX.X)
                    dve.drain()
                    nc.vector.reciprocal(CRC, CSUM)
                    dve.drain()
                    nc.vector.tensor_tensor(EW[:, 2, :].rearrange("p (h k) -> p h k", h=PH), CE,
                                            CRC.unsqueeze(2).broadcast_to([P, PH, TOPK]), ALU.mult)
                    dve.drain().then_inc(tk_ready, 1)
                    dve.wait_ge(ewt_ready, l * TILES + (t + 1))
                    settled(dve)
                    with dve.Fori(0, 16) as i:
                        for b in range(2):
                            dve.wait_ge(gmm_done, l * (32 * TILES) + i * 2 + (32 * t + b + 1))
                            for k in range(4):
                                tok = bass.ds(i * 8 + (4 * b + k), 1)
                                nc.vector.tensor_scalar(HOT[:, b, 2 * k, :], iota, EWT[:, 1, tok], None, ALU.is_equal)
                                last = nc.vector.tensor_scalar(HOT[:, b, 2 * k + 1, :], iota, EWT[:, 0, tok], EWT[:, 2, tok],
                                                               ALU.is_equal, ALU.mult)
                            last.then_inc(hot_ready, 1)
                nc.vector.memset(HF, 0.0)
                phase_end(dve, l, 7)

                def gate_and_add(i, m0, activations):
                    for k in range(4):
                        activations(i, k)
                        if k % 2 == 0:
                            dve.wait_ge(g_in[k // 2], l * (4 * E1) + i * 16 + (4 * m0 + 16))
                        nc.vector.tensor_tensor(HW[:, k, :], HW[:, k, :], GT[:, k, :], ALU.mult)
                        dve.drain()
                        if k % 2 == 0:
                            dve.wait_ge(o_ready, l * (4 * E1) + i * 16 + (4 * (m0 + k) + 8))
                        nc.vector.tensor_copy(HB[:, k, 0, :], HW[:, k, :])
                        dve.drain()
                        nc.vector.tensor_tensor(HB[:, k, 1, :], HW[:, k, :], HB[:, k, 0, :].bitcast(F32), ALU.subtract).then_inc(h_ready, 1)
                    for half in range(2):
                        dve.drain()
                        for d in range(DC):
                            dve.wait_ge(o_ready, l * (4 * E1) + i * 16 + (4 * m0 + 16 + 8 * half + d + 1))
                            nc.vector.tensor_tensor(AC[:, d, :], AC[:, d, :], PF[:, 2048 + 1024 * (d % 2):2048 + 1024 * (d % 2) + TOK],
                                                    ALU.add).then_inc(ac_done, 1)

                def gelu_done(i, k):
                    dve.wait_ge(ge_done, l * E1 + i * 4 + (EARLY + k + 3))

                def gate_step(i, k, step):
                    if step == 0:
                        dve.wait_ge(a_in[k // 2 % 2], l * (4 * EARLY) + i * 16 + (16 * (k // 4) + 16))
                        dve.wait_ge(g_in[k // 2 % 2], l * (4 * E1) + i * 16 + (4 * LATE + 16 * (k // 4) + 16))
                    e = k % 4 + step // 3
                    if step % 3 == 0:
                        nc.vector.tensor_tensor(HW[:, e, :], HW[:, e, :], GT[:, e, :], ALU.mult)
                        return
                    dve.drain()
                    if step % 3 == 1:
                        nc.vector.tensor_copy(HB[:, e, 0, :], HW[:, e, :])
                    else:
                        nc.vector.tensor_tensor(HB[:, e, 1, :], HW[:, e, :], HB[:, e, 0, :].bitcast(F32), ALU.subtract).then_inc(h_ready, 1)

                def add_sums(i, k, gate_next):
                    dve.drain()
                    for d in range(DC):
                        dve.wait_ge(o_ready, l * (4 * E1) + i * 16 + (4 * LATE + 16 + 4 * k + d + 1))
                        nc.vector.tensor_tensor(AC[:, d, :], AC[:, d, :], PF[:, 2048 + 1024 * (d % 2):2048 + 1024 * (d % 2) + TOK],
                                                ALU.add).then_inc(ac_done, 1)
                        if gate_next and d < 6:
                            gate_step(i, k + 2, d)

                with dve.Fori(0, LATE // 4) as i:
                    gate_and_add(i, 0, gelu_done)
                for step in range(6):
                    gate_step(0, 0, step)
                with dve.Fori(0, EARLY // 4 - 1) as i:
                    add_sums(i, 0, True)
                    add_sums(i, 2, True)
                add_sums(EARLY // 4 - 1, 0, True)
                add_sums(EARLY // 4 - 1, 2, False)
                dve.drain()
                for c in range(DC):
                    for g, (lo, hi) in enumerate(((0, LAT), (LAT, TOK))):
                        nc.vector.scalar_tensor_tensor(XT[:, c, lo:hi], AC[:, c, lo:hi], MD4[:, 5, c, g:g + 1],
                                                       XT[:, c, lo:hi], ALU.mult, ALU.add)
                phase_end(dve, l, 8)
                dve.drain().then_inc(layer_free, 1)

        @block.gpsimd
        def _(pool):
            pool.wait_ge(c_in, 32)
            for _ in range(2):
                pool.nop().then_inc(u_split, 1)
                pool.nop().then_inc(v_split, 1)

            def low(dst, src, high, sem_):
                nc.gpsimd.tensor_tensor(dst, src, high.bitcast(F32), ALU.subtract).then_inc(sem_, 1)

            def low_block(l, n):
                m = SPLIT_NO[n]
                pool.wait_ge(hi_ready, l * N_SPLIT + (m + 1))
                low(UR[:, m % 2, 1, :], WR[:, n % RING, 0:D], UR[:, m % 2, 0, :], split)

            with pool.Fori(0, DEPTH) as l:
                def low_h(which):
                    for c in range(DC):
                        pool.wait_ge(hh_ready, l * (2 * DC) + (which * DC + c + 1))
                        low(HR[:, 1, c, :], HT[:, c, :], HR[:, 0, c, :], hr_ready)

                low_block(l, B_FM)
                low_block(l, B_FM + 1)
                phase_end(pool, l, 0)
                low_h(0)

                def cos_part(n):
                    kind, _ = items[n]
                    r = rope_no[n]
                    parts = D_QK if kind in ("dq", "dk") else P
                    tab = {"a": 0, "b": 1, "c": 1, "d": 2}[kind[0]]
                    pool.wait_ge(yn_ready, l * NN + (norm_no[n] + 1))
                    if r == 0:
                        pool.wait_ge(l_in, l * 96 + 80)
                    if r >= 2:
                        pool.wait_ge(rope_done, l * NR + (r - 1))
                    nc.gpsimd.tensor_tensor(T1[0:parts, r % 2, :], YN[0:parts, r % 2, :], TG[0:parts, 2 * tab, :],
                                            ALU.mult).then_inc(t1_ready, 1)

                for s in range(NI + 2):
                    if s < N_FM:
                        low_block(l, B_FM + s + 2)
                    if s == N_FM:
                        for n in range(2, N_V):
                            low_block(l, B_V + n)
                    if s - 2 in rope_no:
                        cos_part(s - 2)
                phase_end(pool, l, 1)

                def low_gate(i, k):
                    m = SPLIT_NO[B_GATE] + k
                    pool.wait_ge(hi_ready, l * N_SPLIT + i * 4 + (m + 1))
                    low(UR[:, m % 2, 1, :], WR[:, k % 4, 0:D], UR[:, m % 2, 0, :], split)

                for k in range(2):
                    low_gate(0, k)
                phase_end(pool, l, 2)
                phase_end(pool, l, 3)
                with pool.Fori(0, DC - 1) as i:
                    for k in range(4):
                        low_gate(i, k + 2)
                for k in range(2):
                    low_gate(DC - 1, k + 2)
                for n in range(2):
                    low_block(l, B_WQ + n)
                phase_end(pool, l, 4)
                phase_end(pool, l, 5)
                low_h(1)
                for n in range(2, N_WQ):
                    low_block(l, B_WQ + n)

                def low_u(i, step, n):
                    pool.wait_ge(uh_ready, l * E1 + i * step + (n + 1))
                    low(UR[:, n % 2, 1, :], WR[:, n % 2, 0:D], UR[:, n % 2, 0, :], u_split)

                def low_v(i, m):
                    pool.wait_ge(vh_ready, l * E1 + i * 4 + (m + 1))
                    low(VR[:, m % 4, 1, :], WR[:, 2 + m % 2, 0:D], VR[:, m % 4, 0, :], v_split)

                low_u(0, 0, 0)
                low_u(0, 0, 1)
                phase_end(pool, l, 6)
                with pool.Fori(0, EARLY // 2) as i:
                    for k in range(2):
                        low_u(i, 2, k + 2)
                phase_end(pool, l, 7)

                def late(i, first, last):
                    for k in range(4):
                        if not last or k < 2:
                            low_u(i, 4, first + EARLY + k + 2)
                        low_v(i, first + k)

                with pool.Fori(0, LATE // 4 - 1) as i:
                    late(i, 0, False)
                late(0, LATE - 4, True)
                with pool.Fori(0, EARLY // 4) as i:
                    for k in range(4):
                        low_v(i, LATE + k)
                phase_end(pool, l, 8)


def key_spans(br, t):
    if t == TILES - 1:
        return [(NEWK, KEYS)]
    if br == "B":
        return [(LAT, NEWK), (P * max(0, t - 1), P * min(4, t + 2))]
    return [(0, LAT), (LAT, NEWK)]


def key_tiles(br, t):
    return [k for lo, hi in key_spans(br, t) for k in range(lo // P, hi // P)]


def make_consts():
    c = np.zeros((P, C_ALL), np.float32)
    i = np.arange(P)
    c[:, C_ONES:C_ONES + P] = 1
    c[:, C_G32:C_G32 + P] = i[:, None] // 32 == i[None] // 32
    c[:, C_G64:C_G64 + P] = i[:, None] // 64 == i[None] // 64

    def rotation(at, size, start, end):
        q = size // 4
        for head in range(start, end, size):
            for half in range(2):
                for r in range(q):
                    x0, x1 = head + half * 2 * q + r, head + half * 2 * q + q + r
                    c[x1, at + x0] = -1
                    c[x0, at + x1] = 1

    rotation(C_RA, A_QK, 0, P)
    rotation(C_RB, HD, 0, P)
    rotation(C_RD, D_ROPE, D_NOPE, D_QK)
    c[:, C_ID:C_ID + P] = np.eye(P)
    c[:, C_PREV:C_PREV + P] = np.where(i[None] >= i[:, None], 0, NEG)
    c[:, C_NEXT:C_NEXT + P] = np.where(i[None] <= i[:, None], 0, NEG)
    c[:, C_IOTA:C_IOTA + P] = i[None]
    for r in range(D_ROPE):
        c[r, C_SEL + D_NOPE + r] = 1
    c[:, C_I16:C_I16 + 16] = np.arange(16)
    c[:, C_EPS] = EPS
    return c


def make_trig():
    out = np.zeros((P, 6, LAT), np.float32)
    tok = np.arange(LAT)
    row, col = (tok // 64).astype(np.float32), (tok % 64).astype(np.float32)
    for n, (size, start, rows) in enumerate(((A_QK, 0, P), (HD, 0, P), (D_ROPE, D_NOPE, D_QK))):
        q = size // 4
        inv = (np.float32(10000.0) ** (-np.arange(q, dtype=np.float32) / np.float32(q))).astype(np.float32)
        out[:, 2 * n] = 1
        for p in range(start, rows):
            f = (p - start) % size
            ang = (row if f < 2 * q else col) * inv[f % q]
            out[p, 2 * n] = np.cos(ang.astype(np.float64))
            out[p, 2 * n + 1] = np.sin(ang.astype(np.float64))
    return out


def blocks_of(w):
    k, n = w.shape
    return np.ascontiguousarray(w.reshape(k // P, P, n // P, P).transpose(2, 1, 0, 3)).reshape(n // P, P, k)


def kernel(**inputs):
    import concourse.bacc as bacc
    from concourse.bass_utils import run_bass_kernel_spmd

    x = {k: np.asarray(v) for k, v in inputs.items()}
    L = DEPTH

    def chunked(v):
        return v.reshape(DC, P).T

    xall = np.concatenate([x["x_sample"][0], x["x_prompt"][0]])
    xT = xall.T.reshape(DC, P, TOK).transpose(1, 0, 2)
    csT = np.stack([chunked(x["c"][0]), chunked(x["c_ctx"])], axis=2).reshape(P, 16)

    sizes = [256, 256, 256, 256, 128, 128, 256, 128, 128, 256, 128, 32, 4096]
    offs = np.concatenate([[0], np.cumsum(sizes)])
    swap = np.concatenate([np.arange(64) + 64 * h for h in (0, 2, 1, 3)])
    ada, wfm, wv, wdq, wkv, wgate, wout, wq, vecs, subk = ([] for _ in range(10))
    for l in range(L):
        ada.append(blocks_of(x["ada_w"][l]))
        aq, ak, av, bq, bk, bv, cq, ck, cv, qa, ckv, kr, gt = (x["w_in"][l][:, offs[i]:offs[i + 1]] for i in range(13))
        kr = np.concatenate([kr, np.zeros((D, P - D_ROPE), np.float32)], axis=1)
        wfm.append(blocks_of(np.concatenate([aq, ak, bq[:, swap], bk, cq[:, swap], ck, qa, ckv, kr], axis=1)))
        v = np.concatenate([av, bv, cv], axis=1)
        wv.append(v.reshape(N_V, 2, P, 512).transpose(0, 2, 1, 3).reshape(N_V, P, 1024))
        wdq.append(x["w_d_qb"][l].reshape(2, P, HEADS * D_QK).transpose(1, 0, 2).reshape(P, -1))
        kv = x["w_d_kvb"][l].reshape(P, HEADS, 128)
        wk = np.concatenate([kv[:, :, :64], np.zeros((P, HEADS, D_ROPE), np.float32)], axis=2).reshape(P, -1)
        wkv.append(np.concatenate([wk, kv[:, :, 64:].reshape(P, -1)], axis=1))
        g = blocks_of(gt).reshape(4, DC, P, D)
        b = x["w_branch"][l].reshape(4, 2, P, DC, P).transpose(3, 0, 2, 1, 4).reshape(DC, 4, P, 2 * P)
        wgate.append(np.concatenate([g.transpose(1, 0, 2, 3), b], axis=3).reshape(N_GATE, P, SLOT))
        wout.append(blocks_of(x["w_out"][l]))
        wq.append(blocks_of(x["peer_wq"][l]))
        subk.append(x["peer_subkeys"][l].transpose(3, 0, 1, 2).reshape(P, SUB, PK))
        lam_init = 0.8 - 0.6 * math.exp(-0.3 * l)
        vec = np.zeros((P, G_ALL), np.float32)
        twice = lambda m: np.repeat(m, 2, axis=1)
        vec[:, G_ADAB:G_ADAB + 96] = twice(x["ada_b"][l].reshape(48, P).T)
        vec[:, G_N1:G_N1 + 16] = twice(chunked(x["norm1_g"][l]))
        vec[:, G_N2:G_N2 + 16] = twice(chunked(x["norm2_g"][l]))
        for c, (name, i, n) in {G_AQ: ("a_qk_g", 0, 4), G_AK: ("a_qk_g", 1, 4), G_BQ: ("b_qk_g", 0, 2), G_BK: ("b_qk_g", 1, 2),
                                G_CQ: ("c_qk_g", 0, 2), G_CK: ("c_qk_g", 1, 2)}.items():
            vec[:, c] = np.tile(x[name][l, i], n)
        vec[:, G_QA:G_QA + 2] = x["d_qnorm_g"][l].reshape(2, P).T
        vec[:, G_CKV] = x["d_kvnorm_g"][l]
        vec[:D_QK, G_DQ] = x["d_qk_g"][l, 0]
        vec[:D_QK, G_DK] = x["d_qk_g"][l, 1]
        vec[:, G_SUB] = np.tile(x["a_subln_g"][l], 2)
        vec[:, G_LAM:G_LAM + 128] = x["a_lam"][l].reshape(1, 128)
        vec[:, G_SINK:G_SINK + 4] = x["b_sink"][l][None]
        vec[:, G_LINIT] = lam_init
        vec[:, G_LREST] = 1.0 - lam_init
        vecs.append(vec)

    def keys_of(name, blocks):
        k = x[name][0].reshape(L, PAST, blocks, P)
        return k.transpose(0, 3, 2, 1)

    cache_k = np.concatenate([keys_of("cache_a_k", 2), keys_of("cache_b_k", 1), keys_of("cache_c_k", 1),
                              keys_of("cache_d_ckv", 1)], axis=2)
    cache_kr = x["cache_d_krope"][0].transpose(0, 2, 1)
    cache_v = np.concatenate([x[f"cache_{b}_v"][0].reshape(L, PAST, -1) for b in "abc"], axis=2)
    uT = x["peer_u"].reshape(L, E1, P, DC, P).transpose(0, 1, 4, 3, 2).reshape(L, E1, P, D)
    vtab = x["peer_v"].reshape(L, E1, P, D)

    ins = dict(xT=xT, csT=csT, consts=make_consts(), trig=make_trig(), vecs=np.stack(vecs), ada=np.stack(ada),
               wfm=np.stack(wfm), wv=np.stack(wv), wdq=np.stack(wdq), wkv=np.stack(wkv), wgate=np.stack(wgate),
               wout=np.stack(wout), wq=np.stack(wq), subk=np.stack(subk), uT=uT, vtab=vtab, cache_k=cache_k,
               cache_kr=cache_kr, cache_v=cache_v)
    outs = dict(yT=(P, DC, TOK), st_k=(L, P, 5, CTX), st_kr=(L, D_ROPE, CTX), st_v=(L, CTX, 512))
    nc = bacc.Bacc("TRN2", target_bir_lowering=False, num_devices=1,
                   dynamic_dma_scratch_size=1024)
    arrays, args = {}, {}
    for name, a in ins.items():
        arrays[f"in_{name}"] = a = np.ascontiguousarray(a)
        args[name] = nc.dram_tensor(f"in_{name}", a.shape, mybir.dt.from_np(a.dtype), kind="ExternalInput").ap()
    for name, shape in outs.items():
        args[name] = nc.dram_tensor(f"out_{name}", shape, F32, kind="ExternalOutput").ap()
    build(nc, **args)
    r = run_bass_kernel_spmd(nc, [arrays], core_ids=[0]).results[0]

    y = r["out_yT"].transpose(1, 0, 2).reshape(D, TOK).T
    sk, skr, sv = r["out_st_k"], r["out_st_kr"], r["out_st_v"]

    def keys(blocks, *shape):
        return sk[:, :, blocks].transpose(0, 3, 2, 1).reshape((1, L, CTX) + shape)

    return (y[LAT:].reshape(1, CTX, D), y[:LAT].reshape(1, LAT, D),
            keys([0, 1], 4, 2, A_QK), sv[:, :, 0:256].reshape(1, L, CTX, 4, 64),
            keys([2], 2, 64), sv[:, :, 256:384].reshape(1, L, CTX, 2, 64),
            keys([3], 2, 64), sv[:, :, 384:512].reshape(1, L, CTX, 2, 64),
            keys([4], 128), skr.transpose(0, 2, 1).reshape(1, L, CTX, D_ROPE))
```
